# Optimizing a Trainium2 kernel written in Bass

```python
import math
import jax, jax.numpy as jnp
from jax import lax
import numpy as np

D_MODEL = 1024
BATCH = 1
SEQ = 1024
DEPTH = 1
DEC_BATCH = 8
DEC_SEQ = 4
PAST_LEN = 8192
PAGE_SIZE = 128

D_A = D_MODEL // 2
H_A = 4
DK = D_A // H_A
DV = D_A // H_A
D_B = D_MODEL - D_A
POOL_WINDOWS = (2, 4, 8, 16)
POOL_GROUP = D_B // len(POOL_WINDOWS)
POOL_HIST = max(POOL_WINDOWS) - 1
D_MIX = D_A + D_B
D_IN = 4 * D_A + D_B
CHUNK = 64
N_EXPERTS = 32
TOP_K = 4
D_FF = 1024
SWIGLU_LIMIT = 7.0
SWIGLU_ALPHA = 1.702
EPS = 1e-6

kernel_name = "hymba_hgrn2_pool_moe_adaln_step"

def rmsnorm(x, w):
    xf = x.astype(jnp.float32)
    y = xf * lax.rsqrt(jnp.mean(xf * xf, axis=-1, keepdims=True) + EPS) * w.astype(jnp.float32)
    return y.astype(x.dtype)

def hgrn2_mix(q, f_pre, i, g, lb, head_norm, S0):
    f32 = jnp.float32
    Bn, T, _ = q.shape
    f = lb.astype(f32) + (1.0 - lb.astype(f32)) * jax.nn.sigmoid(f_pre.astype(f32))
    logf = jnp.log(f)
    k = 1.0 - f
    qa = jax.nn.silu(q.astype(f32))

    def heads(a):
        return a.reshape(Bn, T, H_A, -1).transpose(0, 2, 1, 3)

    qh, kh, gh, vh = heads(qa), heads(k), heads(logf), heads(i.astype(f32))
    C = min(CHUNK, T)
    n = -(-T // C)
    pad = n * C - T

    def chunks(a):
        a = jnp.pad(a, ((0, 0), (0, 0), (0, pad), (0, 0)))
        return a.reshape(Bn, H_A, n, C, a.shape[-1]).transpose(2, 0, 1, 3, 4)

    mask = jnp.tril(jnp.ones((C, C), dtype=bool))[:, :, None]

    def step(S, inp):
        qc, kc, vc, gc = inp
        b = jnp.cumsum(gc, axis=2)
        o_inter = jnp.einsum('bhtk,bhkv->bhtv', qc * jnp.exp(b), S)
        diff = b[:, :, :, None, :] - b[:, :, None, :, :]
        decay = jnp.exp(jnp.where(mask, diff, -jnp.inf))
        A = jnp.einsum('bhtk,bhsk,bhtsk->bhts', qc, kc, decay)
        o = o_inter + jnp.einsum('bhts,bhsv->bhtv', A, vc)
        b_last = b[:, :, -1:, :]
        S_new = jnp.exp(b_last[:, :, 0, :, None]) * S + jnp.einsum(
            'bhsk,bhsv->bhkv', kc * jnp.exp(b_last - b), vc)
        return S_new, o

    S, o = lax.scan(step, S0.astype(f32), (chunks(qh), chunks(kh), chunks(vh), chunks(gh)))
    o = o.transpose(1, 2, 0, 3, 4).reshape(Bn, H_A, n * C, DV)[:, :, :T]
    o = o * lax.rsqrt(jnp.mean(o * o, axis=-1, keepdims=True) + EPS) * head_norm.astype(f32)[None, :, None, :]
    o = o.transpose(0, 2, 1, 3).reshape(Bn, T, D_A) * jax.nn.silu(g.astype(f32))
    return o.astype(q.dtype), S

def pool_mix(v, hist, start, w_pool, pool_scale):
    f32 = jnp.float32
    T = v.shape[1]
    full = jnp.concatenate([hist.astype(v.dtype), v], axis=1)
    cs = jnp.pad(jnp.cumsum(full.astype(f32), axis=1), ((0, 0), (1, 0), (0, 0)))
    pos = start + jnp.arange(T) + 1
    outs = []
    for gi, w in enumerate(POOL_WINDOWS):
        ch = slice(gi * POOL_GROUP, (gi + 1) * POOL_GROUP)
        s = cs[:, POOL_HIST + 1:POOL_HIST + 1 + T, ch] - cs[:, POOL_HIST + 1 - w:POOL_HIST + 1 - w + T, ch]
        cnt = jnp.minimum(pos, w).astype(f32)[None, :, None]
        d = s / cnt - v[:, :, ch].astype(f32)
        outs.append(jnp.einsum('btc,cd->btd', d, w_pool[gi].astype(f32)))
    y = jnp.concatenate(outs, axis=-1) * pool_scale.astype(f32)
    return y.astype(v.dtype), full[:, -POOL_HIST:]

def moe(h, w_router, b_router, w_gu, b_gu, w_down, b_down):
    shp = h.shape
    hf = h.reshape(-1, shp[-1])
    n = hf.shape[0]
    logits = (hf @ w_router + b_router).astype(jnp.float32)
    top_val, top_idx = lax.top_k(logits, TOP_K)
    probs = jax.nn.softmax(top_val, axis=-1)
    flat_e = top_idx.reshape(-1)
    flat_tok = jnp.arange(n * TOP_K) // TOP_K
    order = jnp.argsort(flat_e)
    e_sorted = flat_e[order]
    tok_sorted = flat_tok[order]
    group_sizes = jnp.bincount(flat_e, length=N_EXPERTS).astype(jnp.int32)
    xs = hf[tok_sorted]
    gu = lax.ragged_dot(xs, w_gu, group_sizes) + b_gu[e_sorted]
    gate = jnp.minimum(gu[:, :D_FF], SWIGLU_LIMIT)
    up = jnp.clip(gu[:, D_FF:], -SWIGLU_LIMIT, SWIGLU_LIMIT)
    act = gate * jax.nn.sigmoid(SWIGLU_ALPHA * gate) * (up + 1.0)
    out = lax.ragged_dot(act.astype(w_down.dtype), w_down, group_sizes) + b_down[e_sorted]
    out = out * probs.reshape(-1)[order][:, None].astype(out.dtype)
    y = jax.ops.segment_sum(out, tok_sorted, num_segments=n)
    return y.reshape(shp).astype(h.dtype)

def layer(x, c, S0, hist, start, lb, w_ada, b_ada, norm1, norm2, w_in, hgrn_norm,
          w_pool, pool_scale, w_out, w_router, b_router, w_gu, b_gu, w_down, b_down):
    mod = (jax.nn.silu(c) @ w_ada + b_ada)[:, None, :]
    sh1, sc1, g1, sh2, sc2, g2 = jnp.split(mod, 6, axis=-1)
    h = rmsnorm(x, norm1) * (1 + sc1) + sh1
    u = h @ w_in
    q, f_pre, i, g, v = jnp.split(u, [D_A, 2 * D_A, 3 * D_A, 4 * D_A], axis=-1)
    o_a, S = hgrn2_mix(q, f_pre, i, g, lb, hgrn_norm, S0)
    o_b, new_hist = pool_mix(v, hist, start, w_pool, pool_scale)
    mix = jnp.concatenate([o_a, o_b], axis=-1) @ w_out
    x = x + g1 * mix
    h2 = rmsnorm(x, norm2) * (1 + sc2) + sh2
    x = x + g2 * moe(h2, w_router, b_router, w_gu, b_gu, w_down, b_down)
    return x, S, new_hist

def setup_inputs(seed: int = 0) -> dict:
    key = jax.random.key(seed)
    ks = jax.random.split(key, 24)
    f32 = jnp.float32
    nrm = lambda k, shp, s: jax.random.normal(k, shp, f32) * s
    return {
        "x_prompt": nrm(ks[0], (BATCH, SEQ, D_MODEL), 1.0),
        "x_sample": nrm(ks[1], (DEC_BATCH, DEC_SEQ, D_MODEL), 1.0),
        "state_hgrn": nrm(ks[2], (DEPTH, DEC_BATCH, H_A, DK, DV), 0.5),
        "state_pool": nrm(ks[3], (DEPTH, DEC_BATCH, POOL_HIST, D_B), 1.0),
        "c_prompt": nrm(ks[4], (BATCH, D_MODEL), 1.0),
        "c_sample": nrm(ks[5], (DEC_BATCH, D_MODEL), 1.0),
        "w_ada": nrm(ks[6], (DEPTH, D_MODEL, 6 * D_MODEL), 0.5 * D_MODEL ** -0.5),
        "b_ada": nrm(ks[7], (DEPTH, 6 * D_MODEL), 0.02),
        "norm1": 1.0 + nrm(ks[8], (DEPTH, D_MODEL), 0.02),
        "norm2": 1.0 + nrm(ks[9], (DEPTH, D_MODEL), 0.02),
        "w_in": nrm(ks[10], (DEPTH, D_MODEL, D_IN), D_MODEL ** -0.5),
        "lower_bounds": nrm(ks[11], (DEPTH + 1, D_A), 0.5),
        "hgrn_norm": 1.0 + nrm(ks[12], (DEPTH, H_A, DV), 0.02),
        "w_pool": nrm(ks[13], (DEPTH, len(POOL_WINDOWS), POOL_GROUP, POOL_GROUP), POOL_GROUP ** -0.5),
        "pool_scale": 1.0 + nrm(ks[14], (DEPTH, D_B), 0.1),
        "w_out": nrm(ks[15], (DEPTH, D_MIX, D_MODEL), D_MIX ** -0.5),
        "w_router": nrm(ks[16], (DEPTH, D_MODEL, N_EXPERTS), D_MODEL ** -0.5),
        "b_router": nrm(ks[17], (DEPTH, N_EXPERTS), 0.01),
        "w_gu": nrm(ks[18], (DEPTH, N_EXPERTS, D_MODEL, 2 * D_FF), D_MODEL ** -0.5),
        "b_gu": nrm(ks[19], (DEPTH, N_EXPERTS, 2 * D_FF), 0.02),
        "w_down": nrm(ks[20], (DEPTH, N_EXPERTS, D_FF, D_MODEL), D_FF ** -0.5),
        "b_down": nrm(ks[21], (DEPTH, N_EXPERTS, D_MODEL), 0.02),
        "final_norm": 1.0 + nrm(ks[22], (D_MODEL,), 0.02),
    }

def reference(x_prompt, x_sample, state_hgrn, state_pool, c_prompt, c_sample, w_ada, b_ada,
              norm1, norm2, w_in, lower_bounds, hgrn_norm, w_pool, pool_scale, w_out,
              w_router, b_router, w_gu, b_gu, w_down, b_down, final_norm):
    lbs = jnp.cumsum(jax.nn.softmax(lower_bounds.astype(jnp.float32), axis=0), axis=0)
    yp, ys = x_prompt, x_sample
    S0_prompt = jnp.zeros((x_prompt.shape[0], H_A, DK, DV), jnp.float32)
    hist_prompt = jnp.zeros((x_prompt.shape[0], POOL_HIST, D_B), x_prompt.dtype)
    Sp_l, Hp_l, Ss_l, Hs_l = [], [], [], []
    for l in range(DEPTH):
        params = (w_ada[l], b_ada[l], norm1[l], norm2[l], w_in[l], hgrn_norm[l], w_pool[l],
                  pool_scale[l], w_out[l], w_router[l], b_router[l], w_gu[l], b_gu[l],
                  w_down[l], b_down[l])
        yp, Sp, Hp = layer(yp, c_prompt, S0_prompt, hist_prompt, 0, lbs[l], *params)
        ys, Ss, Hs = layer(ys, c_sample, state_hgrn[l], state_pool[l], PAST_LEN, lbs[l], *params)
        Sp_l.append(Sp.astype(state_hgrn.dtype))
        Hp_l.append(Hp.astype(state_pool.dtype))
        Ss_l.append(Ss.astype(state_hgrn.dtype))
        Hs_l.append(Hs.astype(state_pool.dtype))
    y_prompt = rmsnorm(yp, final_norm)
    y_sample = rmsnorm(ys, final_norm)
    return (y_prompt, y_sample, jnp.stack(Sp_l), jnp.stack(Hp_l), jnp.stack(Ss_l), jnp.stack(Hs_l))


_drawn_inputs = setup_inputs


def setup_inputs(seed=0):
    import zlib

    import numpy as np

    out = dict(_drawn_inputs(seed))
    spreads = {}
    factors = {'norm1': 3.156,
     'norm2': 3.0,
     'hgrn_norm': 5.531,
     'b_router': 20.056,
     'b_gu': 8.0,
     'b_down': 42.403,
     'final_norm': 7.897}
    for name, (base, spread) in spreads.items():
        noise = np.random.default_rng([zlib.crc32(name.encode()), seed]).standard_normal(out[name].shape)
        drawn = base * np.exp(spread * noise) if base else spread * noise
        out[name] = __import__('jax').numpy.asarray(drawn.astype(out[name].dtype))
    for name, factor in factors.items():
        out[name] = (out[name] * factor).astype(out[name].dtype)
    return out
```

```python
from contextlib import ExitStack

import concourse.bass as bass
from concourse import mybir

F32 = mybir.dt.float32
I32 = mybir.dt.int32
U32 = mybir.dt.uint32
ALU = mybir.AluOpType
ACT = mybir.ActivationFunctionType
AX = mybir.AxisListType.X

P = 128
D = 1024
KT = D // P
H = 4
HW = H * P
D_IN = 4 * HW + HW
WINDOWS = (2, 4, 8, 16)
HIST = max(WINDOWS) - 1
NTOK = 1024
NB, TS = 8, 4
NS = NB * TS
TILES = NTOK // P
NT = NTOK + NS
NC = 1 + NB
MODS = 6
SH1, SC1, G1, SH2, SC2, G2 = range(MODS)
E = 32
TOPK = 4
FF = 1024
FT = FF // P
LIMIT = 7.0
ALPHA = 1.702
EPS = 1e-6
ITEM = 256
REGION = -(-NT // ITEM) * ITEM
SLOTS = E * REGION
ITEMS = E + NT * TOPK // ITEM
SIZES = (128, 160, 192, 256)
IDLE = len(SIZES)
BLOCKS = (1, 2, 4, 8, 16, 32, 64)
BLOCKS_S = (1, 2)


class Signals(dict):

    def __init__(self, nc, phase):
        super().__init__()
        self.nc, self.phase = nc, phase

    def __missing__(self, name):
        self[name] = self.nc.alloc_semaphore(f"{self.phase}_{name}")
        return self[name]

    def clear(self):
        self.nc.clear_and_free_semaphores(list(self.values()))
        self.nc.all_engine_barrier()


def modulation(nc, a, scratch):
    NP = MODS * D // 512
    BUF = 3
    s = Signals(nc, "ada")
    with ExitStack() as ctx:
        def sb(name, shape, dt=F32):
            return ctx.enter_context(nc.sbuf_tensor(name, shape, dt))

        wada = [sb(f"wada{j}", [P, KT, 512]) for j in range(BUF)]
        bada = [sb(f"bada{j}", [NC, 512]) for j in range(BUF)]
        modt = [sb(f"modt{j}", [NC, 512]) for j in range(BUF)]
        c9 = sb("c9", [NC, D])
        sig = sb("sig", [NC, D])
        ident = sb("identa", [P, P])
        cT = sb("cT", [P, KT * NC])
        blank = sb("blank", [P, SLOTS // P, 2], I32)
        pt = ctx.enter_context(nc.psum_tensor("pt", [P, 512], F32))
        pm = [ctx.enter_context(nc.psum_tensor(f"pm{j}", [P, 512], F32)) for j in range(BUF)]
        w_view = a["w_ada"][0].rearrange("(k p) n -> p k n", p=P)
        block = ctx.enter_context(nc.Block())

        @block.sync
        def _(sp):
            sp.dma_start(c9[0:1, :], a["c_prompt"]).then_inc(s["c_in"], 16)
            sp.dma_start(c9[1:NC, :], a["c_sample"]).then_inc(s["c_in"], 16)
            with sp.Fori(0, NP // BUF) as i:
                for j in range(BUF):
                    sp.wait_ge(s[f"w_free{j}"], i + 1)
                    sp.wait_ge(s[f"mod_free{j}"], i + 1)
                    cols = bass.ds((i * BUF + j) * 512, 512)
                    sp.dma_start(wada[j][:, :, :], w_view[:, :, cols]).then_inc(s[f"w_in{j}"], 16)
                    sp.dma_start(bada[j][:, :], a["b_ada"][0:1, cols].broadcast_to([NC, 512])).then_inc(s[f"b_in{j}"], 16)

        @block.gpsimd
        def _(pool):
            pool.memset(ident[:, :], 0.0).then_inc(s["ident0"], 1)
            pool.wait_ge(s["ident0"], 1)
            pool.affine_select(out=ident[:, :], in_=ident[:, :], compare_op=ALU.not_equal, fill=1.0,
                               base=0, pattern=[[-1, P]], channel_multiplier=1).then_inc(s["ident"], 1)
            pool.memset(blank[:, :, 0], 0)
            pool.iota(blank[:, :, 1], [[1, SLOTS // P]], base=NT * TOPK, channel_multiplier=SLOTS // P).then_inc(s["blank"], 1)
            pool.wait_ge(s["blank"], 1)
            pool.dma_start(scratch["slots"].rearrange("(p n) c -> p n c", p=P), blank[:, :, :]).then_inc(s["list_out"], 16)
            pool.wait_ge(s["list_out"], 16)

        @block.tensor
        def _(pe):
            for j in range(BUF):
                pe.sem_inc(s[f"w_free{j}"], 1)
            pe.wait_ge(s["ident"], 1)
            pe.wait_ge(s["c_silu"], 1)
            for k in range(KT):
                last = pe.transpose(pt[:, k * NC:(k + 1) * NC], sig[:, k * P:(k + 1) * P], ident[0:NC, 0:NC])
            last.then_inc(s["cT_ps"], 1)
            pe.wait_ge(s["cT"], 1)
            with pe.Fori(0, NP // BUF) as i:
                for j in range(BUF):
                    pe.wait_ge(s[f"w_in{j}"], i * 16 + 16)
                    pe.wait_ge(s[f"mod_free{j}"], i + 1)
                    for k in range(KT):
                        last = pe.matmul(pm[j][0:NC, :], cT[:, k * NC:(k + 1) * NC], wada[j][:, k, :],
                                         start=(k == 0), stop=(k == KT - 1))
                    last.then_inc(s[f"w_free{j}"], 1)

        @block.scalar
        def _(act):
            act.wait_ge(s["c_in"], 32)
            act.activation(sig[:, :], c9[:, :], ACT.Sigmoid).then_inc(s["c_sig"], 1)
            with act.Fori(0, NP // BUF) as i:
                for j in range(BUF):
                    act.wait_ge(s[f"mod{j}"], i + 1)
                    act.dma_start(scratch["mod"][:, bass.ds((i * BUF + j) * 512, 512)], modt[j][:, :]).then_inc(s[f"mod_out{j}"], 16)
            for j in range(BUF):
                act.wait_ge(s[f"mod_out{j}"], 16 * (NP // BUF) + 16)

        @block.vector
        def _(dve):
            for j in range(BUF):
                dve.sem_inc(s[f"mod_free{j}"], 1)
                dve.sem_inc(s[f"mod_out{j}"], 16)
            dve.wait_ge(s["c_sig"], 1)
            dve.tensor_tensor(sig[:, :], sig[:, :], c9[:, :], ALU.mult).then_inc(s["c_silu"], 1)
            dve.wait_ge(s["cT_ps"], 1)
            dve.tensor_copy(cT[:, :], pt[:, 0:KT * NC]).then_inc(s["cT"], 1)
            with dve.Fori(0, NP // BUF) as i:
                for j in range(BUF):
                    dve.wait_ge(s[f"w_free{j}"], i + 2)
                    dve.wait_ge(s[f"b_in{j}"], i * 16 + 16)
                    dve.wait_ge(s[f"mod_out{j}"], i * 16 + 16)
                    dve.tensor_tensor(modt[j][:, :], pm[j][0:NC, :], bada[j][:, :], ALU.add).then_inc(s[f"mod{j}"], 1)
                    dve.engine_nop().then_inc(s[f"mod_free{j}"], 1)
    s.clear()


def mixing(nc, a, scratch, out, keep):
    s = Signals(nc, "mix")
    with ExitStack() as ctx:
        def sb(name, shape, dt=F32):
            return ctx.enter_context(nc.sbuf_tensor(name, shape, dt))

        probs, pdense = keep["probs"], keep["pdense"]
        ident = keep["ident"]
        w_in = sb("w_in", [P, KT, D_IN])
        w_out = sb("w_out", [P, KT, D])
        w_pool = sb("w_pool", [P, H, P])
        w_rt = sb("w_rt", [P, KT, E])
        mul1, add1, gate1, mul2, add2 = (sb(n, [P, D]) for n in ("mul1", "add1", "gate1", "mul2", "add2"))
        hnorm = sb("hnorm", [P, HW])
        b_rt = sb("b_rt", [P, E])
        small = sb("small", [3 * H, P])
        cols = sb("cols", [P, 3 * H])
        lbd = sb("lbd", [P, H])
        lb = sb("lb", [P, H])
        oml = sb("oml", [P, H])
        eps = sb("eps", [P, 1])
        ones = sb("ones", [P, P])
        tri = sb("tri", [P, P])
        masks = [sb(f"mask{i}", [P, P]) for i in range(len(BLOCKS))]
        reset = sb("reset", [P, HW])
        reset_s = sb("reset_s", [P, H * NS])
        seqmask = sb("seqmask", [NS, NB])
        iota_e = sb("iota_e", [P, E])
        iota_i = sb("iota_i", [P, E], I32)
        entries = sb("entries", [P, TILES + 1, TOPK, 2], I32)
        slot0 = sb("slot0", [P, E])
        icnt = sb("icnt", [P, H, P])
        x = sb("x", [P, D])
        h = sb("h", [P, D])
        hT = sb("hT", [P, KT * P])
        f, q, k, lf, b, eb, qb, kend, dk = (sb(n, [P, HW]) for n in ("f", "q", "k", "lf", "b", "eb", "qb", "kend", "dk"))
        sgf, sgq = f, q
        v, gs = sb("v", [P, HW]), sb("gs", [P, HW])
        lev = [sb(f"lev{i}", [P, HW]) for i in range(2)]
        A = sb("A", [P, HW])
        S = sb("S", [P, HW])
        kT = dk
        o = kend
        wd = b
        vx = sb("vx", [P, H, HIST + P])
        pw1 = sb("pw1", [P, 5 * P])
        pw2 = sb("pw2", [P, 5 * P])
        mixT = sb("mixT", [P, KT * P])
        ss = sb("ss", [P, 8])
        rs = sb("rs", [P, 8])
        lg = sb("lg", [P, E])
        top = sb("top", [P, 8])
        topi = sb("topi", [P, 8], U32)
        topf = sb("topf", [P, 8])
        sm = sb("sm", [P, 16])
        hot = sb("hot", [P, TOPK * E])
        hotp = sb("hotp", [P, TOPK * E])
        chosen = sb("chosen", [P, E])
        pos = sb("pos", [P, E])
        slotf = sb("slotf", [P, TOPK])
        slotc = sb("slotc", [P, TOPK], I32)
        entry = sb("entry", [P, TOPK, 2], I32)
        im = {n: sb("im_" + n, [P, E]) for n in ("m", "t", "cum", "le", "lem", "hot")}
        ic = sb("ic", [P, 16])
        tab_f = sb("tab_f", [ITEMS, 4], I32)
        region0 = sb("region0", [P, E])
        iota_pi = sb("iota_pi", [P, 1], I32)
        iota_p = sb("iota_p", [P, 1])
        ramp = sb("ramp", [P, P], I32)
        junk = mixT

        pA, pB, pQ, pF, pV, pI, pG, pW = (ctx.enter_context(nc.psum_tensor(n, [P, 512], F32))
                                          for n in ("pA", "pB", "pQ", "pF", "pV", "pI", "pG", "pW"))
        flat_in = w_in[:, :, :].rearrange("p k n -> p (k n)")
        NBH = NB * H
        S0 = flat_in[:, 0:NBH * P].rearrange("p (b h v) -> p b h v", b=NB, h=H)
        Vz = flat_in[0:NS, NBH * P:2 * NBH * P].rearrange("p (b n) -> p b n", b=NB)
        Qz = flat_in[:, 2 * NBH * P:2 * NBH * P + H * NB * NS]
        hist = flat_in[0:NB * HIST, 3 * NBH * P:3 * NBH * P + HW]
        rest = 3 * NBH * P + HW
        vxs = flat_in[:, rest:rest + H * NB * (HIST + TS)].rearrange("p (h b t) -> p h b t", h=H, b=NB)
        rest += H * NB * (HIST + TS)
        vtc = flat_in[:, rest:rest + H * NS]
        lvl_ps = (pQ, pF)

        block = ctx.enter_context(nc.Block())
        mod = scratch["mod"]
        adds = ((mul1, SC1), (add1, SH1), (gate1, G1), (mul2, SC2), (add2, SH2))

        @block.sync
        def _(sp):
            sp.dma_start(small[0:2 * H, :], a["lower_bounds"].rearrange("r (h p) -> (r h) p", p=P)).then_inc(s["small_in"], 16)
            sp.dma_start(small[2 * H:3 * H, :], a["pool_scale"].rearrange("o (h p) -> (o h) p", p=P)).then_inc(s["small_in"], 16)
            sp.dma_start(x[:, :], a["norm1"].broadcast_to([P, D])).then_inc(s["rows_in"], 16)
            sp.dma_start(h[:, :], a["norm2"].broadcast_to([P, D])).then_inc(s["rows_in"], 16)
            for dst, m in adds:
                sp.dma_start(dst[:, :], mod[0:1, m * D:(m + 1) * D].broadcast_to([P, D])).then_inc(s["rows_in"], 16)
            sp.dma_start(hnorm[:, :], a["hgrn_norm"].rearrange("o h p -> o (h p)").broadcast_to([P, HW])).then_inc(s["rows_in"], 16)
            sp.dma_start(b_rt[:, :], a["b_router"].broadcast_to([P, E])).then_inc(s["rows_in"], 16)
            for j in range(5):
                sp.dma_start(w_in[:, :, j * HW:(j + 1) * HW],
                             a["w_in"][0].rearrange("(k p) n -> p k n", p=P)[:, :, j * HW:(j + 1) * HW]).then_inc(s["w_in"], 16)
            sp.dma_start(w_out[:, :, :], a["w_out"][0].rearrange("(k p) n -> p k n", p=P)).then_inc(s["w_in"], 16)
            sp.dma_start(w_pool[:, :, :], a["w_pool"][0].rearrange("g c d -> c g d")).then_inc(s["w_in"], 16)
            sp.dma_start(w_rt[:, :, :], a["w_router"][0].rearrange("(k p) n -> p k n", p=P)).then_inc(s["w_in"], 16)
            with sp.Fori(0, TILES) as t:
                sp.wait_ge(s["x_free"], t + 1)
                sp.dma_start(x[:, :], a["x_prompt"][0, bass.ds(t * P, P), :]).then_inc(s["x_in"], 16)
                sp.wait_ge(s["x1"], t + 1)
                sp.dma_start(scratch["x1"][bass.ds(t * P, P), :], x[:, :]).then_inc(s["x1_out"], 16)
                sp.wait_ge(s["h2"], t + 1)
                sp.dma_start(scratch["h2"][bass.ds(t * P, P), :], h[:, :]).then_inc(s["h2_out"], 16)
            sp.wait_ge(s["S"], TILES + 1)
            sp.dma_start(out["S_p"][0, 0].rearrange("h k v -> k h v"), S[:, :].rearrange("p (h v) -> p h v", h=H)).then_inc(s["st_out"], 16)
            sp.wait_ge(s["x_free"], TILES + 1)
            sp.wait_ge(s["h2_out"], 16 * (TILES + 1))
            sp.dma_start(x[0:NS, :], a["norm1"].broadcast_to([NS, D])).then_inc(s["rows_s"], 16)
            sp.dma_start(h[0:NS, :], a["norm2"].broadcast_to([NS, D])).then_inc(s["rows_s"], 16)
            for dst, m in adds:
                for j in range(NB):
                    sp.dma_start(dst[j * TS:(j + 1) * TS, :], mod[1 + j:2 + j, m * D:(m + 1) * D].broadcast_to([TS, D])).then_inc(s["rows_s"], 16)
            sp.wait_ge(s["rows_s_set"], 1)
            sp.dma_start(x[0:NS, :], a["x_sample"].rearrange("b t d -> (b t) d")).then_inc(s["x_in"], 16)
            sp.wait_ge(s["g_mm"], TILES + 1)
            sp.dma_start(S0, a["state_hgrn"][0].rearrange("b h k v -> k b h v")).then_inc(s["s0_in"], 16)
            sp.dma_start(hist, a["state_pool"][0].rearrange("b r c -> (b r) c")).then_inc(s["hist_in"], 16)
            sp.dma_start(out["H_s"][0, :, 0:HIST - TS, :], a["state_pool"][0, :, TS:HIST, :]).then_inc(s["st_out"], 16)
            sp.wait_ge(s["x1"], TILES + 1)
            sp.dma_start(scratch["x1"][NTOK:NT, :], x[0:NS, :]).then_inc(s["x1_out"], 16)
            sp.wait_ge(s["h2"], TILES + 1)
            sp.dma_start(scratch["h2"][NTOK:NT, :], h[0:NS, :]).then_inc(s["h2_out"], 16)
            sp.wait_ge(s["S_s"], NBH)
            sp.dma_start(out["S_s"][0].rearrange("b h k v -> k b h v"), S0).then_inc(s["st_out"], 16)
            sp.wait_ge(s["items"], 1)
            sp.dma_start(scratch["table"], tab_f[:, :]).then_inc(s["tab_out"], 16)
            sp.wait_ge(s["tab_out"], 16)
            sp.wait_ge(s["st_out"], 16 * 3)
            sp.wait_ge(s["x1_out"], 16 * (TILES + 1))
            sp.wait_ge(s["h2_out"], 16 * (TILES + 2))

        def pe_tile(pe, t, T, G, blocks, sample):
            done = t + 1

            pe.wait_ge(s["h1"], done)
            for kt in range(KT):
                bank = (pA, pB)[kt // 4]
                last = pe.transpose(bank[:, (kt % 4) * T:(kt % 4 + 1) * T], h[0:T, kt * P:(kt + 1) * P], ident[0:T, 0:T])
            last.then_inc(s["hT_ps"], 1)
            pe.wait_ge(s["hT_lo"], done)
            pe.wait_ge(s["hT_hi"], done)

            for bank, first, name in ((pF, HW, "f_mm"), (pQ, 0, "q_mm"), (pV, 4 * HW, "v_mm")):
                for m in range(H):
                    for kt in range(KT):
                        last = pe.matmul(bank[:, m * T:(m + 1) * T], w_in[:, kt, first + m * P:first + (m + 1) * P],
                                         hT[:, kt * T:(kt + 1) * T], start=(kt == 0), stop=(kt == KT - 1))
                last.then_inc(s[name], 1)
            for bank, first, name in ((pI, 2 * HW, "i_mm"), (pG, 3 * HW, "g_mm")):
                for kt in range(KT):
                    last = pe.matmul(bank[0:T, :], hT[:, kt * T:(kt + 1) * T], w_in[:, kt, first:first + HW],
                                     start=(kt == 0), stop=(kt == KT - 1))
                last.then_inc(s[name], 1)

            if sample:
                pe.wait_ge(s["hist_in"], 16)
                for m in range(H):
                    last = pe.transpose(pB[:, m * NB * HIST:(m + 1) * NB * HIST], hist[:, m * P:(m + 1) * P], ident[0:NB * HIST, 0:NB * HIST])
                last.then_inc(s["hist_ps"], 1)
                pe.wait_ge(s["vtc"], 1)
                for m in range(H):
                    last = pe.transpose(pA[0:NS, m * P:(m + 1) * P], vtc[:, m * NS:(m + 1) * NS], ident[:, :])
                last.then_inc(s["vrow_s_ps"], 1)
                pe.wait_ge(s["vrow_s"], 1)

            pe.wait_ge(s["k"], done)
            pe.wait_ge(s["q"], done)
            for m in range(H):
                last = pe.matmul(pQ[0:T, m * T:(m + 1) * T], k[:, m * T:(m + 1) * T], q[:, m * T:(m + 1) * T],
                                 start=True, stop=True)
            last.then_inc(s["lvl_mm"], 1)
            base, level = t * LV, t * (LV - 1)
            for i in range(len(blocks)):
                pe.wait_ge(s["lev"], level + i + 1)
                if i >= 1:
                    pe.wait_ge(s["lvl"], base + i)
                xl = lev[i % 2]
                for m in range(H):
                    last = pe.matmul(lvl_ps[(i + 1) % 2][0:T, m * T:(m + 1) * T], xl[:, m * T:(m + 1) * T],
                                     xl[:, m * T:(m + 1) * T], start=True, stop=True)
                last.then_inc(s["lvl_mm"], 1)

            pe.wait_ge(s["kend"], done)
            for m in range(H):
                last = pe.transpose(pW[0:T, m * P:(m + 1) * P], kend[:, m * T:(m + 1) * T], ident[:, :])
            last.then_inc(s["kT_ps"], 1)

            pe.wait_ge(s["pool_d"], done)
            for m in range(H):
                last = pe.matmul(pV[:, m * T:(m + 1) * T], w_pool[:, m, :], pw1[:, m * T:(m + 1) * T], start=True, stop=True)
            last.then_inc(s["pool_mm"], 1)

            pe.wait_ge(s["v"], done)
            pe.wait_ge(s["qb"], done)
            pe.wait_ge(s["lvl"], base + len(blocks) + 1)
            if not sample:
                pe.wait_ge(s["S"], done)
                for m in range(H):
                    pe.matmul(pI[0:T, m * P:(m + 1) * P], qb[:, m * T:(m + 1) * T], S[:, m * P:(m + 1) * P], start=True, stop=False)
                    last = pe.matmul(pI[0:T, m * P:(m + 1) * P], A[0:T, m * T:(m + 1) * T], v[0:T, m * P:(m + 1) * P], start=False, stop=True)
                last.then_inc(s["o_mm"], 1)
                pe.wait_ge(s["kT"], done)
                pe.wait_ge(s["gs"], done)
                for m in range(H):
                    last = pe.matmul(pG[:, m * P:(m + 1) * P], kT[0:T, m * P:(m + 1) * P], v[0:T, m * P:(m + 1) * P], start=True, stop=True)
                last.then_inc(s["S_mm"], 1)
            else:
                pe.wait_ge(s["Qz"], 1)
                pe.wait_ge(s["s0_in"], 16)
                for m in range(H):
                    for j in range(NB):
                        pe.matmul(pI[0:T, m * P:(m + 1) * P], Qz[:, (m * NB + j) * NS:(m * NB + j + 1) * NS], S0[:, j, m, :],
                                  start=(j == 0), stop=False)
                    last = pe.matmul(pI[0:T, m * P:(m + 1) * P], A[0:T, m * T:(m + 1) * T], v[0:T, m * P:(m + 1) * P], start=False, stop=True)
                last.then_inc(s["o_mm"], 1)
                pe.wait_ge(s["kT"], done)
                pe.wait_ge(s["Vz"], 1)
                pe.wait_ge(s["gs"], done)
                for j in range(NB):
                    bank = (pG, pF)[j % 2]
                    if j >= 2:
                        pe.wait_ge(s["S_s"], H * (j - 1))
                    for m in range(H):
                        last = pe.matmul(bank[:, m * P:(m + 1) * P], kT[0:T, m * P:(m + 1) * P], Vz[:, j, m * P:(m + 1) * P], start=True, stop=True)
                    last.then_inc(s["S_s_mm"], 1)

            pe.wait_ge(s["o"], done)
            for m in range(H):
                last = pe.transpose(pA[:, m * T:(m + 1) * T], o[0:T, m * P:(m + 1) * P], ident[0:T, 0:T])
            last.then_inc(s["oT_ps"], 1)
            pe.wait_ge(s["oT"], done)
            pe.wait_ge(s["pool_y"], done)
            for n, bank in enumerate((pW, pQ)):
                for kt in range(KT):
                    last = pe.matmul(bank[0:T, :], mixT[:, kt * T:(kt + 1) * T], w_out[:, kt, n * 512:(n + 1) * 512],
                                     start=(kt == 0), stop=(kt == KT - 1))
                last.then_inc(s["out_mm"], 1)

            pe.wait_ge(s["h2"], done)
            for kt in range(KT):
                bank = (pA, pB)[kt // 4]
                last = pe.transpose(bank[:, (kt % 4) * T:(kt % 4 + 1) * T], h[0:T, kt * P:(kt + 1) * P], ident[0:T, 0:T])
            last.then_inc(s["h2T_ps"], 1)
            pe.wait_ge(s["h2T_lo"], done)
            pe.wait_ge(s["h2T_hi"], done)
            for kt in range(KT):
                last = pe.matmul(pI[0:T, 0:E], hT[:, kt * T:(kt + 1) * T], w_rt[:, kt, :], start=(kt == 0), stop=(kt == KT - 1))
            last.then_inc(s["router_mm"], 1)
            pe.wait_ge(s["chosen"], done)
            pe.matmul(pV[0:T, 0:E], tri[0:T, 0:T], chosen[0:T, :], start=True, stop=True)
            pe.matmul(pV[:, E:2 * E], ones[0:T, :], chosen[0:T, :], start=True, stop=True).then_inc(s["rank_mm"], 1)

        LV = len(BLOCKS) + 1

        @block.tensor
        def _(pe):
            pe.wait_ge(s["consts"], 1)
            pe.wait_ge(s["small_in"], 32)
            pe.transpose(pA[:, 0:3 * H], small[:, :], ident[0:3 * H, 0:3 * H]).then_inc(s["cols_ps"], 1)
            pe.wait_ge(s["cols"], 1)
            pe.wait_ge(s["w_in"], 16 * 8)
            with pe.Fori(0, TILES) as t:
                pe_tile(pe, t, P, P, BLOCKS, False)
            pe.wait_ge(s["rank_used"], TILES)
            for m in range(H):
                last = pe.transpose(pB[:, m * P:(m + 1) * P], vx[:, m, HIST:HIST + P], ident[:, :])
            last.then_inc(s["vrow_ps"], 1)
            pe.wait_ge(s["vrow"], 1)
            pe_tile(pe, TILES, NS, TS, BLOCKS_S, True)

        def act_norm(act, src, T, col, done, tag):
            act.activation(junk[0:T, :], src, ACT.Square,
                           accum_out=ss[0:T, col:col + 1]).then_inc(s["ss" + tag], 1)
            act.wait_ge(s["ss" + tag], done)
            act.activation(rs[0:T, col:col + 1], ss[0:T, col:col + 1], ACT.Ln, scale=1.0 / D, bias=eps[0:T, :]).then_inc(s["ln" + tag], 1)
            act.wait_ge(s["ln" + tag], done)
            act.activation(rs[0:T, col:col + 1], rs[0:T, col:col + 1], ACT.Exp, scale=-0.5).then_inc(s["r" + tag], 1)

        def act_tile(act, t, T, G, blocks, sample):
            done = t + 1
            n = H * T
            act.wait_ge(s["x_in"], 16 * done if isinstance(t, int) else t * 16 + 16)
            act_norm(act, x[0:T, :], T, 0, done, "1")
            act.wait_ge(s["hT_ps"], done)
            act.activation(hT[:, 0:4 * T], pA[:, 0:4 * T], ACT.Copy).then_inc(s["hT_lo"], 1)
            act.wait_ge(s["f_mm"], done)
            act.activation(sgf[:, 0:n], pF[:, 0:n], ACT.Sigmoid).then_inc(s["sgf"], 1)
            act.wait_ge(s["q_mm"], done)
            act.activation(sgq[:, 0:n], pQ[:, 0:n], ACT.Sigmoid).then_inc(s["sgq"], 1)
            act.wait_ge(s["v_mm"], done)
            if not sample:
                act.wait_ge(s["carried"], done)
                act.activation(vx[:, :, HIST:HIST + T], pV[:, 0:n].rearrange("p (h t) -> p h t", h=H), ACT.Copy).then_inc(s["vx"], 1)
            act.wait_ge(s["i_mm"], done)
            act.activation(v[0:T, :], pI[0:T, :], ACT.Copy).then_inc(s["v"], 1)
            act.wait_ge(s["g_mm"], done)
            act.activation(gs[0:T, :], pG[0:T, :], ACT.Sigmoid).then_inc(s["sgg"], 1)
            if sample:
                act.activation(vtc, pV[:, 0:n], ACT.Copy).then_inc(s["vtc"], 1)
                act.activation(vxs[:, :, :, HIST:HIST + TS], pV[:, 0:n].rearrange("p (h b t) -> p h b t", h=H, b=NB), ACT.Copy)
                act.wait_ge(s["hist_ps"], 1)
                act.activation(vxs[:, :, :, 0:HIST], pB[:, 0:H * NB * HIST].rearrange("p (h b t) -> p h b t", h=H, b=NB), ACT.Copy).then_inc(s["vx"], 1)
                act.wait_ge(s["vrow_s_ps"], 1)
                act.activation(junk[0:NS, 0:HW], pA[0:NS, :], ACT.Copy).then_inc(s["vrow_s"], 1)
                act.wait_ge(s["vrow_s"], 1)
                for j in range(NB):
                    act.dma_start(out["H_s"][0, j, HIST - TS:HIST, :], junk[j * TS:(j + 1) * TS, 0:HW]).then_inc(s["vrow_out"], 16)
                act.wait_ge(s["vrow_out"], 16 + 16 * NB)
            act.wait_ge(s["f"], done)
            act.activation(lf[:, 0:n], f[:, 0:n], ACT.Ln).then_inc(s["lf"], 1)
            act.wait_ge(s["b"], done)
            act.activation(eb[:, 0:n], b[:, 0:n], ACT.Exp).then_inc(s["eb"], 1)
            act.wait_ge(s["dk"], done)
            act.activation(dk[:, 0:n], dk[:, 0:n], ACT.Exp).then_inc(s["ek"], 1)
            level = t * (LV - 1)
            for i in range(len(blocks)):
                act.wait_ge(s["dlev"], level + i + 1)
                act.activation(lev[i % 2][:, 0:n], lev[i % 2][:, 0:n], ACT.Exp).then_inc(s["elev"], 1)
            act.wait_ge(s["kT_ps"], done)
            act.activation(kT[0:T, :], pW[0:T, :], ACT.Copy).then_inc(s["kT"], 1)
            act.wait_ge(s["o_mm"], done)
            for m in range(H):
                last = act.activation(junk[0:T, m * P:(m + 1) * P], pI[0:T, m * P:(m + 1) * P], ACT.Square,
                                      accum_out=ss[0:T, 2 + m:3 + m])
            last.then_inc(s["sso"], 1)
            act.wait_ge(s["sso"], done)
            act.activation(rs[0:T, 2:2 + H], ss[0:T, 2:2 + H], ACT.Ln, scale=1.0 / P, bias=eps[0:T, :]).then_inc(s["lno"], 1)
            act.wait_ge(s["lno"], done)
            act.activation(rs[0:T, 2:2 + H], rs[0:T, 2:2 + H], ACT.Exp, scale=-0.5).then_inc(s["ro"], 1)
            act.wait_ge(s["oT_ps"], done)
            act.activation(mixT[:, 0:n], pA[:, 0:n], ACT.Copy).then_inc(s["oT"], 1)
            act.wait_ge(s["x1"], done)
            act_norm(act, x[0:T, :], T, 1, done, "2")
            act.wait_ge(s["h2T_ps"], done)
            act.activation(hT[:, 0:4 * T], pA[:, 0:4 * T], ACT.Copy).then_inc(s["h2T_lo"], 1)
            act.wait_ge(s["nmax"], done)
            act.activation(sm[0:T, 1:5], top[0:T, 0:TOPK], ACT.Exp, bias=sm[0:T, 0:1], accum_out=sm[0:T, 5:6]).then_inc(s["etop"], 1)

        @block.scalar
        def _(act):
            act.wait_ge(s["lbd"], 1)
            act.activation(lb[:, :], lbd[:, :], ACT.Sigmoid).then_inc(s["lb"], 1)
            act.wait_ge(s["consts"], 1)
            with act.Fori(0, TILES) as t:
                act_tile(act, t, P, P, BLOCKS, False)
            act.wait_ge(s["vrow_ps"], 1)
            act.activation(junk[:, 0:HW], pB[:, :], ACT.Copy).then_inc(s["vrow"], 1)
            act.wait_ge(s["vrow"], 1)
            act.dma_start(out["H_p"][0, 0], junk[P - HIST:P, 0:HW]).then_inc(s["vrow_out"], 16)
            act.wait_ge(s["vrow_out"], 16)
            act_tile(act, TILES, NS, TS, BLOCKS_S, True)

        def halves(ap, B):
            w = ap.rearrange("p (j two c) -> p j two c", two=2, c=B)
            return w[:, :, 0, :], w[:, :, 1, :], w[:, :, 0, B - 1:B]

        def dve_tile(dve, t, T, G, blocks, sample):
            done = t + 1
            n = H * T
            dve.wait_ge(s["r1"], done)
            if not sample:
                dve.wait_ge(s["h2_out"], t * 16 + 16)
            dve.scalar_tensor_tensor(out=h[0:T, :], in0=x[0:T, :], scalar=rs[0:T, 0:1], in1=mul1[0:T, :], op0=ALU.mult, op1=ALU.mult).then_inc(s["h0"], 1)
            dve.wait_ge(s["h0"], done)
            dve.tensor_tensor(h[0:T, :], h[0:T, :], add1[0:T, :], ALU.add).then_inc(s["h1"], 1)
            dve.wait_ge(s["hT_ps"], done)
            dve.tensor_copy(hT[:, 4 * T:8 * T], pB[:, 0:4 * T]).then_inc(s["hT_hi"], 1)
            dve.wait_ge(s["sgf"], done)
            for m in range(H):
                last = dve.tensor_scalar(f[:, m * T:(m + 1) * T], sgf[:, m * T:(m + 1) * T], oml[:, m:m + 1], lb[:, m:m + 1], ALU.mult, ALU.add)
            last.then_inc(s["f"], 1)
            dve.wait_ge(s["sgq"], done)
            dve.tensor_tensor(q[:, 0:n], sgq[:, 0:n], pQ[:, 0:n], ALU.mult).then_inc(s["q"], 1)
            dve.wait_ge(s["lf"], done)
            rmask = reset_s if sample else reset
            dve.tensor_tensor_scan(b[:, 0:n], rmask[:, 0:n], lf[:, 0:n], 0.0, ALU.mult, ALU.add).then_inc(s["b"], 1)
            dve.wait_ge(s["b"], done)
            bg = b[:, 0:n].rearrange("p (g c) -> p g c", c=G)
            dve.tensor_tensor(dk[:, 0:n].rearrange("p (g c) -> p g c", c=G), bg[:, :, G - 1:G].broadcast_to([P, n // G, G]), bg, ALU.subtract).then_inc(s["dk"], 1)
            dve.wait_ge(s["sgg"], done)
            dve.tensor_tensor(gs[0:T, :], gs[0:T, :], pG[0:T, :], ALU.mult).then_inc(s["gs"], 1)

            base = t * LV

            def take(i):
                dve.wait_ge(s["lvl_mm"], base + i + 1)
                if i:
                    dve.wait_ge(s["lvl"], base + i)
                dve.sem_inc(s["met"], 1)
                mask = ident if i == 0 else masks[i - 1]
                dve.copy_predicated(A[0:T, 0:n].rearrange("p (h t) -> p h t", h=H),
                                    mask[0:T, 0:T].bitcast(I32).unsqueeze(1).broadcast_to([T, H, T]),
                                    (pQ if i == 0 else lvl_ps[i % 2])[0:T, 0:n].rearrange("p (h t) -> p h t", h=H)).then_inc(s["lvl"], 1)

            for i, B in enumerate(blocks):
                if i >= 2:
                    dve.wait_ge(s["lvl_mm"], base + i)
                left, right, border = halves(b[:, 0:n], B)
                dl, dr, _ = halves(lev[i % 2][:, 0:n], B)
                dve.tensor_tensor(dl, border.broadcast_to(list(left.shape)), left, ALU.subtract)
                dve.tensor_tensor(dr, right, border.broadcast_to(list(left.shape)), ALU.subtract).then_inc(s["dlev"], 1)
                if i == 1:
                    take(0)
                if i >= 2:
                    take(i - 1)
            take(len(blocks) - 1)
            take(len(blocks))

            if not sample:
                dve.wait_ge(s["S_mm"], done)
                for m in range(H):
                    last = dve.scalar_tensor_tensor(out=S[:, m * P:(m + 1) * P], in0=S[:, m * P:(m + 1) * P], scalar=eb[:, (m + 1) * T - 1:(m + 1) * T],
                                                    in1=pG[:, m * P:(m + 1) * P], op0=ALU.mult, op1=ALU.add)
                last.then_inc(s["S"], 1)
            dve.wait_ge(s["ro"], done)
            dve.wait_ge(s["gn"], done)
            for m in range(H):
                last = dve.scalar_tensor_tensor(out=o[0:T, m * P:(m + 1) * P], in0=pI[0:T, m * P:(m + 1) * P], scalar=rs[0:T, 2 + m:3 + m],
                                                in1=gs[0:T, m * P:(m + 1) * P], op0=ALU.mult, op1=ALU.mult)
            last.then_inc(s["o"], 1)
            dve.wait_ge(s["pool_mm"], done)
            for m in range(H):
                last = dve.tensor_scalar(mixT[:, n + m * T:n + (m + 1) * T], pV[:, m * T:(m + 1) * T], cols[:, 2 * H + m:2 * H + m + 1], None, ALU.mult)
            last.then_inc(s["pool_y"], 1)
            if sample:
                for j in range(NB):
                    dve.wait_ge(s["S_s_mm"], j + 1)
                    bank = (pG, pF)[j % 2]
                    for m in range(H):
                        c = m * NS + j * TS + TS - 1
                        dve.scalar_tensor_tensor(out=S0[:, j, m, :], in0=S0[:, j, m, :], scalar=eb[:, c:c + 1],
                                                 in1=bank[:, m * P:(m + 1) * P], op0=ALU.mult, op1=ALU.add).then_inc(s["S_s"], 1)
            for j, bank in enumerate((pW, pQ)):
                dve.wait_ge(s["out_mm"], 2 * t + j + 1)
                last = dve.tensor_tensor(h[0:T, j * 512:(j + 1) * 512], bank[0:T, :], gate1[0:T, j * 512:(j + 1) * 512], ALU.mult)
            last.then_inc(s["gated"], 1)
            dve.wait_ge(s["gated"], done)
            dve.tensor_tensor(x[0:T, :], x[0:T, :], h[0:T, :], ALU.add).then_inc(s["x1"], 1)
            dve.wait_ge(s["r2"], done)
            dve.scalar_tensor_tensor(out=h[0:T, :], in0=x[0:T, :], scalar=rs[0:T, 1:2], in1=mul2[0:T, :], op0=ALU.mult, op1=ALU.mult).then_inc(s["h20"], 1)
            dve.wait_ge(s["h20"], done)
            dve.tensor_tensor(h[0:T, :], h[0:T, :], add2[0:T, :], ALU.add).then_inc(s["h2"], 1)
            dve.wait_ge(s["h2T_ps"], done)
            dve.tensor_copy(hT[:, 4 * T:8 * T], pB[:, 0:4 * T]).then_inc(s["h2T_hi"], 1)
            dve.wait_ge(s["router_mm"], done)
            dve.tensor_tensor(lg[0:T, :], pI[0:T, 0:E], b_rt[0:T, :], ALU.add).then_inc(s["lg"], 1)
            dve.wait_ge(s["lg"], done)
            dve.sem_inc(s["met"], 1)
            dve.max(top[0:T, :], lg[0:T, :]).then_inc(s["top"], 1)
            dve.wait_ge(s["top"], done)
            dve.tensor_scalar(sm[0:T, 0:1], top[0:T, 0:1], -1.0, None, ALU.mult).then_inc(s["nmax"], 1)
            dve.max_index(topi[0:T, :], top[0:T, :], lg[0:T, :]).then_inc(s["topi"], 1)
            dve.wait_ge(s["topi"], done)
            dve.tensor_copy(topf[0:T, :], topi[0:T, :]).then_inc(s["topf"], 1)
            dve.wait_ge(s["etop"], done)
            dve.reciprocal(sm[0:T, 6:7], sm[0:T, 5:6]).then_inc(s["rsum"], 1)
            dve.wait_ge(s["rsum"], done)
            pr = probs[0:T, bass.ds(t, 1), :] if not isinstance(t, int) else probs[0:T, t:t + 1, :]
            dve.tensor_scalar(sm[0:T, 8:12], sm[0:T, 1:5], sm[0:T, 6:7], None, ALU.mult).then_inc(s["prob"], 1)
            dve.wait_ge(s["topf"], done)
            dve.wait_ge(s["prob"], done)
            dve.tensor_copy(pr, sm[0:T, 8:12].unsqueeze(1))
            for c in range(TOPK):
                dve.tensor_scalar(hot[0:T, c * E:(c + 1) * E], iota_e[0:T, :], topf[0:T, c:c + 1], None, ALU.is_equal)
                last = dve.tensor_scalar(hotp[0:T, c * E:(c + 1) * E], iota_e[0:T, :], topf[0:T, c:c + 1], sm[0:T, 8 + c:9 + c], ALU.is_equal, ALU.mult)
            last.then_inc(s["hot"], 1)
            dve.wait_ge(s["hot"], done)
            dve.tensor_reduce(chosen[0:T, :], hot[0:T, :].rearrange("p (c e) -> p e c", c=TOPK), AX, ALU.add).then_inc(s["chosen"], 1)
            pd = pdense[0:T, bass.ds(t, 1), :] if not isinstance(t, int) else pdense[0:T, t:t + 1, :]
            dve.tensor_reduce(pos[0:T, :], hotp[0:T, :].rearrange("p (c e) -> p e c", c=TOPK), AX, ALU.add).then_inc(s["pd"], 1)
            dve.wait_ge(s["pd"], done)
            dve.tensor_copy(pd, pos[0:T, :].unsqueeze(1)).then_inc(s["pd_kept"], 1)
            dve.wait_ge(s["rank_mm"], done)
            dve.wait_ge(s["pd_kept"], done)
            dve.tensor_tensor(pos[0:T, :], pV[0:T, 0:E], slot0[0:T, :], ALU.add).then_inc(s["pos"], 1)
            dve.wait_ge(s["pos"], done)
            dve.tensor_tensor(hot[0:T, :].rearrange("p (c e) -> p c e", c=TOPK), hot[0:T, :].rearrange("p (c e) -> p c e", c=TOPK),
                              pos[0:T, :].unsqueeze(1).broadcast_to([T, TOPK, E]), ALU.mult).then_inc(s["hotpos"], 1)
            dve.tensor_tensor(slot0[:, :], slot0[:, :], pV[:, E:2 * E], ALU.add).then_inc(s["rank_used"], 1)
            dve.wait_ge(s["hotpos"], done)
            dve.tensor_reduce(slotf[0:T, :], hot[0:T, :].rearrange("p (c e) -> p c e", c=TOPK), AX, ALU.add).then_inc(s["slotf"], 1)
            dve.wait_ge(s["slotf"], done)
            dve.wait_ge(s["slotc_free"], done)
            en = entries[:, bass.ds(t, 1)] if not isinstance(t, int) else entries[:, t:t + 1]
            dve.tensor_copy(entry[:, :, :].rearrange("p c w -> p (c w)"), en.rearrange("p o c w -> p (o c w)"))
            dve.tensor_copy(slotc[0:T, :], slotf[0:T, :]).then_inc(s["slotc"], 1)

        @block.vector
        def _(dve):
            dve.sem_inc(s["h2_out"], 16)
            dve.sem_inc(s["slotc_free"], 1)
            dve.wait_ge(s["cnt"], 1)
            dve.reciprocal(icnt[:, :, :], icnt[:, :, :]).then_inc(s["icnt_r"], 1)
            dve.memset(eps[:, :], EPS)
            dve.memset(A[:, :], 0.0)
            dve.memset(S[:, :], 0.0).then_inc(s["S"], 1)
            dve.wait_ge(s["cols_ps"], 1)
            dve.tensor_copy(cols[:, :], pA[:, 0:3 * H]).then_inc(s["cols"], 1)
            dve.wait_ge(s["cols"], 1)
            dve.tensor_tensor(lbd[:, :], cols[:, 0:H], cols[:, H:2 * H], ALU.subtract).then_inc(s["lbd"], 1)
            dve.wait_ge(s["lb"], 1)
            dve.tensor_scalar(oml[:, :], lb[:, :], -1.0, 1.0, ALU.mult, ALU.add)
            dve.wait_ge(s["rows_in"], 16 * 9)
            dve.scalar_tensor_tensor(out=mul1[:, :], in0=mul1[:, :], scalar=1.0, in1=x[:, :], op0=ALU.add, op1=ALU.mult)
            dve.scalar_tensor_tensor(out=mul2[:, :], in0=mul2[:, :], scalar=1.0, in1=h[:, :], op0=ALU.add, op1=ALU.mult).then_inc(s["x_free"], 1)
            dve.wait_ge(s["x_free"], 1)
            dve.wait_ge(s["consts"], 1)
            with dve.Fori(0, TILES) as t:
                dve_tile(dve, t, P, P, BLOCKS, False)
                dve.wait_ge(s["x1_out"], t * 16 + 16)
                dve.sem_inc(s["x_free"], 1)
            dve.wait_ge(s["rows_s"], 16 * (2 + 5 * NB))
            dve.scalar_tensor_tensor(out=mul1[0:NS, :], in0=mul1[0:NS, :], scalar=1.0, in1=x[0:NS, :], op0=ALU.add, op1=ALU.mult)
            dve.scalar_tensor_tensor(out=mul2[0:NS, :], in0=mul2[0:NS, :], scalar=1.0, in1=h[0:NS, :], op0=ALU.add, op1=ALU.mult).then_inc(s["rows_s_set"], 1)
            dve.wait_ge(s["rows_s_set"], 1)
            dve.memset(A[0:NS, 0:H * NS], 0.0)
            dve_tile(dve, TILES, NS, TS, BLOCKS_S, True)

            M = ITEMS
            dve.wait_ge(s["rank_used"], TILES + 1)
            cnt = pos
            dve.wait_ge(s["slotc"], TILES + 1)
            dve.tensor_tensor(cnt[:, :], slot0[:, :], region0[:, :], ALU.subtract).then_inc(s["im0"], 1)
            dve.wait_ge(s["im0"], 1)
            dve.tensor_scalar(im["m"][:, :], cnt[:, :], 0.0, None, ALU.is_gt).then_inc(s["im0"], 1)
            step = 2
            for c in range(1, REGION // ITEM):
                dve.tensor_scalar(im["t"][:, :], cnt[:, :], float(c * ITEM), None, ALU.is_gt).then_inc(s["im0"], 1)
                step += 1
                dve.wait_ge(s["im0"], step)
                dve.tensor_tensor(im["m"][:, :], im["m"][:, :], im["t"][:, :], ALU.add).then_inc(s["im0"], 1)
                step += 1
                dve.wait_ge(s["im0"], step)
            dve.tensor_tensor_scan(im["cum"][:, :], ones[:, 0:E], im["m"][:, :], 0.0, ALU.mult, ALU.add).then_inc(s["im1"], 1)
            dve.wait_ge(s["im1"], 1)
            dve.tensor_scalar(im["le"][0:M, :], im["cum"][0:M, :], iota_p[0:M, 0:1], None, ALU.is_le).then_inc(s["im1"], 1)
            dve.wait_ge(s["im1"], 2)
            dve.tensor_reduce(ic[0:M, 0:1], im["le"][0:M, :], AX, ALU.add)
            dve.tensor_tensor(im["lem"][0:M, :], im["le"][0:M, :], im["m"][0:M, :], ALU.mult).then_inc(s["im1"], 1)
            dve.wait_ge(s["im1"], 3)
            dve.tensor_reduce(ic[0:M, 1:2], im["lem"][0:M, :], AX, ALU.add)
            dve.tensor_scalar(im["hot"][0:M, :], iota_e[0:M, :], ic[0:M, 0:1], None, ALU.is_equal).then_inc(s["im1"], 1)
            dve.wait_ge(s["im1"], 4)
            dve.tensor_tensor(ic[0:M, 2:3], iota_p[0:M, 0:1], ic[0:M, 1:2], ALU.subtract)
            dve.tensor_tensor(im["hot"][0:M, :], im["hot"][0:M, :], cnt[0:M, :], ALU.mult).then_inc(s["im1"], 1)
            dve.wait_ge(s["im1"], 5)
            dve.tensor_reduce(ic[0:M, 3:4], im["hot"][0:M, :], AX, ALU.add)
            dve.tensor_scalar(ic[0:M, 4:5], ic[0:M, 2:3], float(ITEM), None, ALU.mult).then_inc(s["im1"], 1)
            dve.wait_ge(s["im1"], 6)
            dve.tensor_tensor(ic[0:M, 5:6], ic[0:M, 3:4], ic[0:M, 4:5], ALU.subtract).then_inc(s["im1"], 1)
            dve.wait_ge(s["im1"], 7)
            dve.scalar_tensor_tensor(out=ic[0:M, 6:7], in0=ic[0:M, 0:1], scalar=float(REGION), in1=ic[0:M, 4:5], op0=ALU.mult, op1=ALU.add)
            dve.tensor_scalar(ic[0:M, 7:8], ic[0:M, 0:1], float(E), float(IDLE), ALU.is_equal, ALU.mult)
            dve.tensor_scalar(ic[0:M, 8:9], ic[0:M, 5:6], float(SIZES[0]), None, ALU.is_gt).then_inc(s["im1"], 1)
            step = 8
            for size in SIZES[1:-1]:
                dve.wait_ge(s["im1"], step)
                dve.tensor_tensor(ic[0:M, 7:8], ic[0:M, 7:8], ic[0:M, 8:9], ALU.add).then_inc(s["im1"], 1)
                dve.wait_ge(s["im1"], step + 1)
                dve.tensor_scalar(ic[0:M, 8:9], ic[0:M, 5:6], float(size), None, ALU.is_gt).then_inc(s["im1"], 1)
                step += 2
            dve.wait_ge(s["im1"], step)
            dve.tensor_tensor(ic[0:M, 7:8], ic[0:M, 7:8], ic[0:M, 8:9], ALU.add).then_inc(s["im1"], 1)
            dve.wait_ge(s["im1"], step + 1)
            dve.tensor_copy(tab_f[:, 0:1], ic[0:M, 7:8])
            dve.tensor_copy(tab_f[:, 1:2], ic[0:M, 0:1])
            dve.tensor_copy(tab_f[:, 3:4], im["cum"][0:M, E - 1:E])
            dve.tensor_copy(tab_f[:, 2:3], ic[0:M, 6:7]).then_inc(s["items"], 1)

        def pool_tile(pool, t, T, G, blocks, sample):
            done = t + 1
            n = H * T
            pool.wait_ge(s["f"], done)
            pool.sem_inc(s["met"], 1)
            pool.tensor_scalar(k[:, 0:n], f[:, 0:n], -1.0, 1.0, ALU.mult, ALU.add).then_inc(s["k"], 1)
            pool.wait_ge(s["q"], done)
            pool.wait_ge(s["eb"], done)
            pool.tensor_tensor(qb[:, 0:n], q[:, 0:n], eb[:, 0:n], ALU.mult).then_inc(s["qb"], 1)
            pool.wait_ge(s["ek"], done)
            pool.wait_ge(s["k"], done)
            pool.tensor_tensor(kend[:, 0:n], k[:, 0:n], dk[:, 0:n], ALU.mult).then_inc(s["kend"], 1)
            level = t * (LV - 1)
            for i, B in enumerate(blocks):
                pool.wait_ge(s["elev"], level + i + 1)
                l, r, _ = halves(lev[i % 2][:, 0:n], B)
                kl, _, _ = halves(k[:, 0:n], B)
                _, qr, _ = halves(q[:, 0:n], B)
                pool.tensor_tensor(l, l, kl, ALU.mult)
                pool.tensor_tensor(r, r, qr, ALU.mult).then_inc(s["lev"], 1)
            pool.wait_ge(s["vx"], done)
            nb, tt = (NB, TS) if sample else (1, P)
            src = vxs if sample else vx[:, :, :].unsqueeze(2)
            bufs = (pw1, pw2)
            groups = []
            width = HIST + tt
            cur = src
            for g, w in enumerate(WINDOWS):
                sh = w // 2
                nw = width - sh
                dst = bufs[g % 2][:, 0:(H - g) * nb * nw].rearrange("p (h b t) -> p h b t", b=nb, t=nw)
                c = cur if g == 0 else cur[:, 1:]
                if g:
                    pool.wait_ge(s["win"], 4 * t + g)
                pool.tensor_tensor(dst, c[:, :, :, sh:width], c[:, :, :, 0:nw], ALU.add).then_inc(s["win"], 1)
                pool.wait_ge(s["win"], 4 * t + g + 1)
                d_out = wd[:, g * T:(g + 1) * T].rearrange("p (b t) -> p b t", b=nb)
                ic_v = icnt[:, g, 0:T].rearrange("p (b t) -> p b t", b=nb)
                pool.tensor_tensor(d_out, dst[:, 0, :, nw - tt:nw], ic_v, ALU.mult).then_inc(s["mean"], 1)
                cur, width = dst, nw
            pool.wait_ge(s["mean"], 4 * t + 4)
            pool.tensor_tensor(pw1[:, 0:n].rearrange("p (h b t) -> p h b t", h=H, b=nb), wd[:, 0:n].rearrange("p (h b t) -> p h b t", h=H, b=nb),
                               src[:, :, :, HIST:HIST + tt], ALU.subtract).then_inc(s["pool_d"], 1)
            if not sample:
                pool.wait_ge(s["pool_d"], done)
                pool.sem_inc(s["met"], 1)
                for g, w in enumerate(WINDOWS):
                    last = pool.memset(icnt[:, g, :], 1.0 / w)
                last.then_inc(s["icnt"], 1)
                pool.wait_ge(s["icnt"], done)
            pool.wait_ge(s["gs"], done)
            pool.tensor_tensor(gs[0:T, :], gs[0:T, :], hnorm[0:T, :], ALU.mult).then_inc(s["gn"], 1)
            if sample:
                pool.wait_ge(s["g_mm"], done)
                pool.memset(Qz, 0.0).then_inc(s["Qz0"], 1)
                pool.wait_ge(s["Qz0"], 1)
                pool.wait_ge(s["qb"], done)
                for j in range(NB):
                    last = pool.tensor_copy(Qz.rearrange("p (h b t) -> p h b t", h=H, b=NB)[:, :, j, j * TS:(j + 1) * TS],
                                            qb[:, 0:n].rearrange("p (h t) -> p h t", h=H)[:, :, j * TS:(j + 1) * TS])
                last.then_inc(s["Qz"], 1)
                pool.wait_ge(s["v"], done)
                for j in range(NB):
                    last = pool.tensor_scalar(Vz[:, j, :], v[0:NS, :], seqmask[:, j:j + 1], 0.0, ALU.mult, ALU.add)
                last.then_inc(s["Vz"], 1)
            pool.wait_ge(s["slotc"], done)
            pool.sem_inc(s["met"], 1)
            for c in range(TOPK):
                pool.indirect_dma_start(scratch["slots"][:, :], bass.IndirectOffsetOnAxis(ap=slotc[0:T, c:c + 1], axis=0),
                                        entry[0:T, c, :], None).then_inc(s["listed"], 16)
            pool.wait_ge(s["listed"], 64 * t + 64)
            pool.sem_inc(s["slotc_free"], 1)

        @block.gpsimd
        def _(pool):
            pool.memset(ident[:, :], 0.0)
            pool.memset(ones[:, :], 1.0)
            pool.memset(tri[:, :], 1.0)
            pool.memset(reset[:, :], 1.0)
            pool.memset(reset_s[:, :], 1.0)
            pool.memset(seqmask[:, :], 1.0)
            for m in masks:
                last = pool.memset(m[:, :], 0.0)
            last.then_inc(s["c0"], 1)
            pool.wait_ge(s["c0"], 1)
            pool.affine_select(out=ident[:, :], in_=ident[:, :], compare_op=ALU.not_equal, fill=1.0,
                               base=0, pattern=[[-1, P]], channel_multiplier=1)
            pool.affine_select(out=tri[:, :], in_=tri[:, :], compare_op=ALU.is_gt, fill=0.0,
                               base=0, pattern=[[1, P]], channel_multiplier=-1)
            pool.memset(reset[:, :].rearrange("p (h t) -> p h t", h=H)[:, :, 0:1], 0.0)
            pool.memset(reset_s[:, :].rearrange("p (g t) -> p g t", t=TS)[:, :, 0:1], 0.0)
            pool.affine_select(out=seqmask[:, :], in_=seqmask[:, :], compare_op=ALU.is_ge, fill=0.0,
                               base=0, pattern=[[-TS, NB]], channel_multiplier=1).then_inc(s["c0"], 1)
            pool.wait_ge(s["c0"], 2)
            pool.affine_select(out=seqmask[:, :], in_=seqmask[:, :], compare_op=ALU.is_ge, fill=0.0,
                               base=TS - 1, pattern=[[TS, NB]], channel_multiplier=-1)
            rights = [(B, m[:, :].rearrange("p (j two c) -> p j two c", two=2, c=B)[:, :, 1, :]) for B, m in zip(BLOCKS, masks)]
            for B, r in rights:
                last = pool.memset(r, 1.0)
            last.then_inc(s["c0"], 1)
            pool.wait_ge(s["c0"], 3)
            for B, r in rights:
                last = pool.affine_select(out=r, in_=r, compare_op=ALU.is_ge, fill=0.0, base=0,
                                          pattern=[[-2 * B, P // (2 * B)], [0, B]], channel_multiplier=1)
            last.then_inc(s["c0"], 1)
            pool.wait_ge(s["c0"], 4)
            for B, r in rights:
                last = pool.affine_select(out=r, in_=r, compare_op=ALU.is_ge, fill=0.0, base=B - 1,
                                          pattern=[[2 * B, P // (2 * B)], [0, B]], channel_multiplier=-1)
            pool.iota(iota_i[:, :], [[1, E]], base=0, channel_multiplier=0)
            pool.iota(entries[:, :, :, 0], [[P, TILES + 1], [0, TOPK]], base=0, channel_multiplier=1)
            pool.iota(entries[:, :, :, 1], [[P * TOPK, TILES + 1], [1, TOPK]], base=0, channel_multiplier=TOPK)
            pool.iota(iota_pi[:, :], [[0, 1]], base=0, channel_multiplier=1)
            pool.iota(ramp[:, :], [[1, P]], base=1, channel_multiplier=0).then_inc(s["c0"], 1)
            pool.memset(vx[:, :, :], 0.0).then_inc(s["c0"], 1)
            pool.wait_ge(s["c0"], 6)
            pool.tensor_copy(iota_e[:, :], iota_i[:, :])
            pool.tensor_copy(iota_p[:, :], iota_pi[:, :])
            pool.tensor_copy(wd[:, 0:P], ramp[:, :]).then_inc(s["c0"], 1)
            pool.wait_ge(s["c0"], 7)
            pool.tensor_scalar(slot0[:, :], iota_e[:, :], float(REGION), 0.0, ALU.mult, ALU.add)
            pool.tensor_scalar(region0[:, :], iota_e[:, :], float(REGION), 0.0, ALU.mult, ALU.add)
            for g, w in enumerate(WINDOWS):
                last = pool.tensor_scalar(icnt[:, g, :], wd[:, 0:P], float(w), 1.0, ALU.min, ALU.mult)
            last.then_inc(s["cnt"], 1)
            pool.wait_ge(s["icnt_r"], 1)
            pool.engine_nop().then_inc(s["consts"], 1)
            pool.sem_inc(s["carried"], 1)
            with pool.Fori(0, TILES) as t:
                pool_tile(pool, t, P, P, BLOCKS, False)
                pool.tensor_copy(vx[:, :, 0:HIST], vx[:, :, P:P + HIST]).then_inc(s["carried"], 1)
            pool_tile(pool, TILES, NS, TS, BLOCKS_S, True)
            pool.wait_ge(s["listed"], 64 * (TILES + 1))
    s.clear()


def experts(nc, a, scratch):
    s = Signals(nc, "moe")
    with ExitStack() as ctx:
        def sb(name, shape, dt=F32):
            return ctx.enter_context(nc.sbuf_tensor(name, shape, dt))

        def ps(name):
            return ctx.enter_context(nc.psum_tensor(name, [P, 512], F32))

        GP = FF // 256
        DP = 2
        wgu = [sb(f"wgu{j}", [P, 2, KT, 256]) for j in range(GP)]
        wdn = [sb(f"wdn{j}", [P, FT // DP, D]) for j in range(DP)]
        table = sb("table", [1, ITEMS * 4], I32)
        identm = sb("identm", [P, P])
        idx = sb("idx", [P, 2, 2], I32)
        xg = [sb(f"xg{m}", [P, D]) for m in range(2)]
        xT = sb("xT", [P, KT, ITEM])
        brow = sb("brow", [2 * FT, P])
        bcol = sb("bcol", [P, 2 * FT])
        gate = [sb(f"gatem{j}", [P, ITEM]) for j in range(2)]
        sig = [sb(f"sigm{j}", [P, ITEM]) for j in range(2)]
        up = [sb(f"up{j}", [P, ITEM]) for j in range(2)]
        glu = [sb(f"glu{j}", [P, ITEM]) for j in range(2)]
        actT = sb("actT", [P, FT, ITEM])
        y = [sb(f"y{m}", [P, D]) for m in range(2)]
        pt = [ps("pt0"), ps("pt1")]
        pg = [ps("pg0"), ps("pg1")]
        pu = [ps("pu0"), ps("pu1")]
        py = [ps("py0"), ps("py1")]
        block = ctx.enter_context(nc.Block())
        gu_view = a["w_gu"][0].rearrange("e (k p) (u n) -> e u p k n", p=P, u=2)
        dn_view = a["w_down"][0].rearrange("e (k p) n -> e p k n", p=P)
        bgu_view = a["b_gu"][0].rearrange("e (j p) -> e j p", p=P)

        def field(eng, i, c, top):
            return eng.value_load(table[0:1, bass.ds(i * 4 + c, 1)], min_val=0, max_val=top)

        def per_class(eng, body):
            eng.wait_ge(s["table"], 16)
            with eng.Fori(0, ITEMS) as i:
                cls = field(eng, i, 0, IDLE)
                for v, n in enumerate(SIZES):
                    with eng.If(cls == v):
                        body(i, n)

        @block.sync
        def _(sp):
            sp.dma_start(table[:, :], scratch["table"].rearrange("i c -> (i c)").unsqueeze(0)).then_inc(s["table"], 16)
            sp.wait_ge(s["table"], 16)
            with sp.Fori(0, ITEMS) as i:
                cls = field(sp, i, 0, IDLE)
                with sp.If(cls < IDLE):
                    e = field(sp, i, 1, E - 1)
                    sp.wait_ge(s["bcol_ps"], i + 1)
                    sp.dma_start(brow[:, :], bgu_view[bass.ds(e, 1)].rearrange("o j p -> (o j) p")).then_inc(s["brow"], 16)
                    for j in range(GP):
                        sp.wait_ge(s["up_mm"], i * FT + 2 * j + 2)
                        for u in range(2):
                            sp.dma_start(wgu[j][:, u, :, :], gu_view[bass.ds(e, 1), u, :, :, j * 256:(j + 1) * 256].rearrange("o p k n -> (o p) k n")).then_inc(s[f"wgu{j}"], 16)
                    for j in range(DP):
                        sp.wait_ge(s["y_mm1"], i * 2 + 2)
                        sp.dma_start(wdn[j][:, :, :], dn_view[bass.ds(e, 1), :, j * FT // DP:(j + 1) * FT // DP, :].rearrange("o p k n -> (o p) k n")).then_inc(s[f"wdn{j}"], 16)

        @block.gpsimd
        def _(pool):
            pool.memset(identm[:, :], 0.0).then_inc(s["ident0"], 1)
            pool.wait_ge(s["ident0"], 1)
            pool.affine_select(out=identm[:, :], in_=identm[:, :], compare_op=ALU.not_equal, fill=1.0,
                               base=0, pattern=[[-1, P]], channel_multiplier=1).then_inc(s["ident"], 1)

            def gather(i, first):
                pool.wait_ge(s["xT_ps1"], i * 2 + 2)
                for m in range(2):
                    pool.dma_start(idx[:, m, :], scratch["slots"][bass.ds(first + m * P, P), :]).then_inc(s["idx"], 16)
                pool.wait_ge(s["idx"], i * 32 + 32)
                pool.sem_inc(s["met"], 1)
                for m in range(2):
                    pool.indirect_dma_start(xg[m][:, :], None, scratch["h2"][:, :],
                                            bass.IndirectOffsetOnAxis(ap=idx[:, m, 0:1], axis=0)).then_inc(s["xg"], 16)

            def item(i, n):
                gather(i, field(pool, i, 2, SLOTS - ITEM))
                for j in range(FT):
                    pool.wait_ge(s["sig"], i * FT + j + 1)
                    pool.tensor_tensor(glu[j % 2][:, 0:n], gate[j % 2][:, 0:n], sig[j % 2][:, 0:n], ALU.mult).then_inc(s["glu"], 1)
                for m, rows_m in enumerate((min(P, n), n - P)):
                    if rows_m:
                        pool.wait_ge(s["y0"], 2 * i + m + 2)
                        pool.wait_ge(s["y1"], 2 * i + m + 2)
                        pool.sem_inc(s["met"], 1)
                        pool.indirect_dma_start(scratch["y"][:, :], bass.IndirectOffsetOnAxis(ap=idx[0:rows_m, m, 1:2], axis=0),
                                                y[m][0:rows_m, :], None, bounds_check=NT * TOPK - 1, oob_is_err=False)\
                            .then_inc(s["y_out"], 32 if n == P else 16)
                pool.wait_ge(s["y_out"], i * 32 + 32)
                pool.sem_inc(s["y_free"], 1)

            pool.sem_inc(s["y_free"], 1)
            per_class(pool, item)

        @block.tensor
        def _(pe):
            pe.sem_inc(s["bcol_ps"], 1)
            pe.sem_inc(s["xT_ps1"], 2)
            pe.sem_inc(s["up_mm"], FT)
            pe.sem_inc(s["y_mm1"], 2)
            pe.wait_ge(s["ident"], 1)

            def item(i, n):
                rows = [min(P, n), n - P]
                pe.wait_ge(s["xg"], i * 32 + 32)
                for g in range(4):
                    m, half = g // 2, g % 2
                    if g >= 2:
                        pe.wait_ge(s[f"xT{half}"], 2 * i + m)
                    for c in range(4):
                        last = pe.transpose(pt[half][:, c * P:(c + 1) * P], xg[m][:, (half * 4 + c) * P:(half * 4 + c + 1) * P], identm[:, :])
                    last.then_inc(s[f"xT_ps{half}"], 1)
                pe.wait_ge(s["brow"], i * 16 + 16)
                pe.wait_ge(s["xT0"], 2 * i + 2)
                pe.wait_ge(s["xT1"], 2 * i + 2)
                pe.sem_inc(s["met"], 1)
                pe.transpose(pt[0][:, 0:2 * FT], brow[:, :], identm[0:2 * FT, 0:2 * FT]).then_inc(s["bcol_ps"], 1)
                for j in range(FT):
                    if j % 2 == 0:
                        pe.wait_ge(s[f"wgu{j // 2}"], i * 32 + 32)
                    pe.wait_ge(s["gate_up_read"], i * FT + j + 1)
                    for u, bank in ((0, pg[j % 2]), (1, pu[j % 2])):
                        for kt in range(KT):
                            last = pe.matmul(bank[:, 0:n], wgu[j // 2][:, u, kt, (j % 2) * P:(j % 2 + 1) * P], xT[:, kt, 0:n],
                                             start=(kt == 0), stop=(kt == KT - 1))
                        last.then_inc(s[("gate_mm", "up_mm")[u]], 1)
                pe.wait_ge(s["act"], i * FT + FT)
                for m, rows_m in enumerate(rows):
                    for half in range(2):
                        if rows_m == 0:
                            continue
                        pe.wait_ge(s[f"y{half}"], 2 * i + m + 1)
                        for ft in range(FT):
                            if m == 0 and half == 0 and ft % (FT // DP) == 0:
                                pe.wait_ge(s[f"wdn{ft // (FT // DP)}"], i * 16 + 16)
                            last = pe.matmul(py[half][0:rows_m, :], actT[:, ft, m * P:m * P + rows_m],
                                             wdn[ft // (FT // DP)][:, ft % (FT // DP), half * 512:(half + 1) * 512],
                                             start=(ft == 0), stop=(ft == FT - 1))
                        last.then_inc(s[f"y_mm{half}"], 2 if n == P else 1)
            per_class(pe, item)

        @block.scalar
        def _(act):
            def item(i, n):
                for m in range(2):
                    act.wait_ge(s["xT_ps0"], 2 * i + m + 1)
                    act.activation(xT[:, 0:4, m * P:(m + 1) * P], pt[0][:, :].rearrange("p (k t) -> p k t", k=4), ACT.Copy).then_inc(s["xT0"], 1)
                for j in range(FT):
                    act.wait_ge(s["gate"], i * FT + j + 1)
                    act.activation(sig[j % 2][:, 0:n], gate[j % 2][:, 0:n], ACT.Sigmoid, scale=ALPHA).then_inc(s["sig"], 1)
                    act.wait_ge(s["up_mm"], i * FT + FT + j + 1)
                    act.activation(up[j % 2][:, 0:n], pu[j % 2][:, 0:n], ACT.Identity, bias=bcol[:, FT + j:FT + j + 1]).then_inc(s["up"], 1)
                act.wait_ge(s["y_free"], i + 1)
                for m, rows_m in enumerate((min(P, n), n - P)):
                    if rows_m == 0:
                        continue
                    whole = 2 if n == P else 1
                    act.wait_ge(s["y_mm0"], 2 * i + m + 1)
                    act.activation(y[m][0:rows_m, 0:512], py[0][0:rows_m, :], ACT.Copy).then_inc(s["y0"], whole)

            act.sem_inc(s["y0"], 1)
            per_class(act, item)

        @block.vector
        def _(dve):
            dve.sem_inc(s["gate_up_read"], 2)
            dve.sem_inc(s["y1"], 1)

            def item(i, n):
                for m in range(2):
                    dve.wait_ge(s["xT_ps1"], 2 * i + m + 3)
                    dve.tensor_copy(xT[:, 4:8, m * P:(m + 1) * P], pt[1][:, :].rearrange("p (k t) -> p k t", k=4)).then_inc(s["xT1"], 1)
                dve.wait_ge(s["bcol_ps"], i + 2)
                dve.tensor_copy(bcol[:, :], pt[0][:, 0:2 * FT]).then_inc(s["bcol"], 1)
                dve.wait_ge(s["bcol"], i + 1)

                def finish(j):
                    dve.wait_ge(s["up"], i * FT + j + 1)
                    dve.tensor_scalar(up[j % 2][:, 0:n], up[j % 2][:, 0:n], -LIMIT, LIMIT, ALU.max, ALU.min).then_inc(s["clip"], 1)
                    dve.wait_ge(s["clip"], i * FT + j + 1)
                    dve.wait_ge(s["glu"], i * FT + j + 1)
                    dve.scalar_tensor_tensor(out=actT[:, j, 0:n], in0=up[j % 2][:, 0:n], scalar=1.0, in1=glu[j % 2][:, 0:n],
                                             op0=ALU.add, op1=ALU.mult).then_inc(s["act"], 1)

                for j in range(FT):
                    dve.wait_ge(s["gate_mm"], i * FT + j + 1)
                    dve.tensor_scalar(gate[j % 2][:, 0:n], pg[j % 2][:, 0:n], bcol[:, j:j + 1], LIMIT, ALU.add, ALU.min).then_inc(s["gate"], 1)
                    if j:
                        finish(j - 1)
                    dve.wait_ge(s["up"], i * FT + j + 1)
                    dve.wait_ge(s["gate"], i * FT + j + 1)
                    dve.sem_inc(s["gate_up_read"], 1)
                finish(FT - 1)
                for m, rows_m in enumerate((min(P, n), n - P)):
                    if rows_m == 0:
                        continue
                    dve.wait_ge(s["y_mm1"], 2 * i + m + 3)
                    dve.wait_ge(s["y_free"], i + 1)
                    dve.tensor_copy(y[m][0:rows_m, 512:1024], py[1][0:rows_m, :]).then_inc(s["y1"], 2 if n == P else 1)

            per_class(dve, item)
    s.clear()


def combination(nc, a, scratch, out, keep):
    with ExitStack() as ctx:
        def sb(name, shape, dt=F32):
            return ctx.enter_context(nc.sbuf_tensor(name, shape, dt))

        def two(name, shape, dt=F32):
            return [sb(f"{name}{j}", shape, dt) for j in range(2)]

        s = Signals(nc, "cmb")
        probs, pdense, ident = keep["probs"], keep["pdense"], keep["ident"]
        gate2, gate2_s, fnorm = sb("gate2", [P, D]), sb("gate2_s", [NS, D]), sb("fnorm", [P, D])
        bdown = sb("bdown", [E, D])
        eps = sb("epsc", [P, 1])
        pr, pd, pT = two("pr", [P, TOPK]), two("pd", [P, E]), two("pT", [E, P])
        yk = two("yk", [P, TOPK, D])
        x1, acc, res, sq = two("x1c", [P, D]), two("acc", [P, D]), two("res", [P, D]), sb("sq", [P, D])
        ss, r = two("ssc", [P, 1]), two("rc", [P, 1])
        ppT = [ctx.enter_context(nc.psum_tensor(f"ppT{j}", [P, 512], F32)) for j in range(2)]
        pb = [[ctx.enter_context(nc.psum_tensor(f"pb{j}{c}", [P, 512], F32)) for c in range(2)] for j in range(2)]
        block = ctx.enter_context(nc.Block())

        PAIRS = TILES // 2

        def all_tiles(eng, body, T_last=NS):
            with eng.Fori(0, PAIRS) as i:
                for u in range(2):
                    body(i, u, P, i * 2 + u, False)
            body(PAIRS, 0, T_last, TILES, True)

        def pick(ap, t, T):
            return ap[0:T, t:t + 1, :] if isinstance(t, int) else ap[0:T, bass.ds(t, 1), :]

        @block.sync
        def _(sp):
            sp.dma_start(gate2[:, :], scratch["mod"][0:1, G2 * D:].broadcast_to([P, D])).then_inc(s["rows"], 16)
            for j in range(NB):
                sp.dma_start(gate2_s[j * TS:(j + 1) * TS, :], scratch["mod"][1 + j:2 + j, G2 * D:].broadcast_to([TS, D])).then_inc(s["rows"], 16)
            sp.dma_start(fnorm[:, :], a["final_norm"].unsqueeze(0).broadcast_to([P, D])).then_inc(s["rows"], 16)
            sp.dma_start(bdown[:, :], a["b_down"][0]).then_inc(s["rows"], 16)

            def tile(i, u, T, t, sample):
                sp.wait_ge(s[f"sum{u}"], i + 1)
                rows = scratch["y"].rearrange("(t c) d -> t (c d)", c=TOPK)
                sp.dma_start(yk[u][0:T, :, :].rearrange("p c d -> p (c d)"), rows[NTOK:NT, :] if sample else rows[bass.ds(t * P, P), :]).then_inc(s[f"yk{u}"], 16)
                src = scratch["x1"][NTOK:NT, :] if sample else scratch["x1"][bass.ds(t * P, P), :]
                sp.dma_start(x1[u][0:T, :], src).then_inc(s[f"x1{u}"], 16)

            all_tiles(sp, tile)

        @block.gpsimd
        def _(pool):
            for u in range(2):
                pool.sem_inc(s[f"sum{u}"], 1)

            def tile(i, u, T, t, sample):
                g = gate2_s if sample else gate2
                pool.wait_ge(s["rows"], 16 * (NB + 3))
                pool.wait_ge(s[f"weighed{u}"], i + 1)
                pool.tensor_tensor(acc[u][0:T, :], acc[u][0:T, :], g[0:T, :], ALU.mult).then_inc(s[f"gated{u}"], 1)
                pool.wait_ge(s[f"gated{u}"], i + 1)
                pool.wait_ge(s[f"x1{u}"], i * 16 + 16)
                pool.tensor_tensor(acc[u][0:T, :], acc[u][0:T, :], x1[u][0:T, :], ALU.add).then_inc(s[f"sum{u}"], 1)

            all_tiles(pool, tile)

        @block.tensor
        def _(pe):
            pe.wait_ge(s["rows"], 16 * (NB + 3))

            def tile(i, u, T, t, sample):
                pe.wait_ge(s[f"picked{u}"], i + 1)
                pe.transpose(ppT[u][0:E, 0:T], pd[u][0:T, :], ident[0:T, 0:T]).then_inc(s[f"pT_ps{u}"], 1)
                pe.wait_ge(s[f"pT{u}"], i + 1)
                for c in range(2):
                    last = pe.matmul(pb[u][c][0:T, :], pT[u][:, 0:T], bdown[:, c * 512:(c + 1) * 512], start=True, stop=True)
                last.then_inc(s[f"bias{u}"], 1)

            all_tiles(pe, tile)

        @block.scalar
        def _(act):
            for u in range(2):
                act.sem_inc(s[f"out{u}"], 16)

            def tile(i, u, T, t, sample):
                act.wait_ge(s[f"pT_ps{u}"], i + 1)
                act.activation(pT[u][:, 0:T], ppT[u][0:E, 0:T], ACT.Copy).then_inc(s[f"pT{u}"], 1)
                act.wait_ge(s["epsc"], 1)
                act.wait_ge(s[f"sum{u}"], i + 2)
                act.activation(sq[0:T, :], acc[u][0:T, :], ACT.Square, accum_out=ss[u][0:T, :]).then_inc(s[f"ss{u}"], 1)
                act.wait_ge(s[f"ss{u}"], i + 1)
                act.activation(r[u][0:T, :], ss[u][0:T, :], ACT.Ln, scale=1.0 / D, bias=eps[0:T, :]).then_inc(s[f"ln{u}"], 1)
                act.wait_ge(s[f"ln{u}"], i + 1)
                act.activation(r[u][0:T, :], r[u][0:T, :], ACT.Exp, scale=-0.5).then_inc(s[f"r{u}"], 1)
                act.wait_ge(s[f"res{u}"], i + 1)
                dst = out["y_s"].rearrange("b t d -> (b t) d") if sample else out["y_p"][0, bass.ds(t * P, P), :]
                act.dma_start(dst, res[u][0:T, :]).then_inc(s[f"out{u}"], 16)

            all_tiles(act, tile)
            act.wait_ge(s["out0"], 16 * (PAIRS + 2))
            act.wait_ge(s["out1"], 16 * (PAIRS + 1))

        @block.vector
        def _(dve):
            dve.memset(eps[:, :], EPS).then_inc(s["epsc"], 1)
            dve.wait_ge(s["rows"], 16 * (NB + 3))

            def tile(i, u, T, t, sample):
                dve.tensor_copy(pr[u][0:T, :].unsqueeze(1), pick(probs, t, T))
                dve.tensor_copy(pd[u][0:T, :].unsqueeze(1), pick(pdense, t, T)).then_inc(s[f"picked{u}"], 1)
                dve.wait_ge(s[f"picked{u}"], i + 1)
                dve.wait_ge(s[f"bias{u}"], i + 1)
                dve.wait_ge(s[f"yk{u}"], i * 16 + 16)
                for c in range(2):
                    last = dve.scalar_tensor_tensor(out=acc[u][0:T, c * 512:(c + 1) * 512], in0=yk[u][0:T, 0, c * 512:(c + 1) * 512], scalar=pr[u][0:T, 0:1],
                                                    in1=pb[u][c][0:T, :], op0=ALU.mult, op1=ALU.add)
                last.then_inc(s[f"part{u}"], 1)
                for c in range(1, TOPK):
                    dve.wait_ge(s[f"part{u}"], i * (TOPK - 1) + c)
                    last = dve.scalar_tensor_tensor(out=acc[u][0:T, :], in0=yk[u][0:T, c, :], scalar=pr[u][0:T, c:c + 1],
                                                    in1=acc[u][0:T, :], op0=ALU.mult, op1=ALU.add)
                    last.then_inc(s[f"part{u}" if c < TOPK - 1 else f"weighed{u}"], 1)
                dve.wait_ge(s[f"r{u}"], i + 1)
                dve.wait_ge(s[f"out{u}"], i * 16 + 16)
                dve.scalar_tensor_tensor(out=res[u][0:T, :], in0=acc[u][0:T, :], scalar=r[u][0:T, 0:1], in1=fnorm[0:T, :],
                                         op0=ALU.mult, op1=ALU.mult).then_inc(s[f"res{u}"], 1)

            all_tiles(dve, tile)


def build(nc, a, out):
    def dram(name, shape, dt=F32):
        return nc.dram_tensor(name, shape, dt, kind="Internal").ap()

    scratch = {
        "mod": dram("mod", (NC, MODS * D)),
        "x1": dram("x1_rows", (NT, D)),
        "h2": dram("h2_rows", (NT, D)),
        "slots": dram("slots", (SLOTS, 2), I32),
        "table": dram("item_table", (ITEMS, 4), I32),
        "y": dram("expert_rows", (NT * TOPK, D)),
    }
    with ExitStack() as ctx:
        keep = {
            "probs": ctx.enter_context(nc.sbuf_tensor("probs", [P, TILES + 1, TOPK], F32)),
            "pdense": ctx.enter_context(nc.sbuf_tensor("pdense", [P, TILES + 1, E], F32)),
            "ident": ctx.enter_context(nc.sbuf_tensor("ident", [P, P], F32)),
        }
        modulation(nc, a, scratch)
        mixing(nc, a, scratch, out, keep)
        experts(nc, a, scratch)
        combination(nc, a, scratch, out, keep)


OUTPUTS = {
    "y_p": (1, NTOK, D), "y_s": (NB, TS, D), "S_p": (1, 1, H, P, P), "H_p": (1, 1, HIST, HW),
    "S_s": (1, NB, H, P, P), "H_s": (1, NB, HIST, HW),
}


def kernel(**inputs):
    import numpy as np
    import concourse.bacc as bacc
    from concourse.bass_utils import run_bass_kernel_spmd

    nc = bacc.Bacc("TRN2", target_bir_lowering=False, num_devices=1)
    arrays, a = {}, {}
    for name, value in inputs.items():
        arrays["in_" + name] = np.ascontiguousarray(value)
        a[name] = nc.dram_tensor("in_" + name, arrays["in_" + name].shape, F32, kind="ExternalInput").ap()
    out = {name: nc.dram_tensor("out_" + name, shape, F32, kind="ExternalOutput").ap() for name, shape in OUTPUTS.items()}
    build(nc, a, out)
    r = run_bass_kernel_spmd(nc, [arrays], core_ids=[0]).results[0]
    return tuple(r["out_" + name] for name in OUTPUTS)
```

```python
from contextlib import ExitStack

import concourse.bass as bass
from concourse import mybir

F32 = mybir.dt.float32
F32R = mybir.dt.float32r
I32 = mybir.dt.int32
U32 = mybir.dt.uint32
ALU = mybir.AluOpType
ACT = mybir.ActivationFunctionType
AX = mybir.AxisListType.X

P = 128
D = 1024
KT = D // P
H = 4
HW = H * P
D_IN = 4 * HW + HW
WINDOWS = (2, 4, 8, 16)
HIST = max(WINDOWS) - 1
NTOK = 1024
NB, TS = 8, 4
NS = NB * TS
TILES = NTOK // P
NT = NTOK + NS
NC = 1 + NB
MODS = 6
SH1, SC1, G1, SH2, SC2, G2 = range(MODS)
E = 32
TOPK = 4
FF = 1024
FT = FF // P
LIMIT = 7.0
ALPHA = 1.702
EPS = 1e-6
ITEM = 256
REGION = -(-NT // ITEM) * ITEM
SLOTS = E * REGION
ITEMS = E + NT * TOPK // ITEM
SIZES = (128, 136, 144, 152, 160, 168, 176, 192, 208, 224, 256)
IDLE = len(SIZES)
BLOCKS = (1, 2, 4, 8, 16, 32, 64)
BLOCKS_S = (1, 2)


class Signals(dict):

    def __init__(self, nc, phase):
        super().__init__()
        self.nc, self.phase = nc, phase

    def __missing__(self, name):
        self[name] = self.nc.alloc_semaphore(f"{self.phase}_{name}")
        return self[name]

    def clear(self):
        self.nc.clear_and_free_semaphores(list(self.values()))
        self.nc.all_engine_barrier()


def first_tile(t):
    return isinstance(t, int) and t == 0


def modulation(nc, a, scratch):
    NP = MODS * D // 512
    BUF = 3
    s = Signals(nc, "ada")
    with ExitStack() as ctx:
        def sb(name, shape, dt=F32):
            return ctx.enter_context(nc.sbuf_tensor(name, shape, dt))

        wada = [sb(f"wada{j}", [P, KT, 512]) for j in range(BUF)]
        bada = [sb(f"bada{j}", [NC, 512]) for j in range(BUF)]
        modt = [sb(f"modt{j}", [NC, 512]) for j in range(BUF)]
        c9 = sb("c9", [NC, D])
        sig = sb("sig", [NC, D])
        ident = sb("identa", [P, P])
        cT = sb("cT", [P, KT * NC])
        blank = sb("blank", [P, SLOTS // P, 2], I32)
        pt = ctx.enter_context(nc.psum_tensor("pt", [P, 512], F32))
        pm = [ctx.enter_context(nc.psum_tensor(f"pm{j}", [P, 512], F32)) for j in range(BUF)]
        w_view = a["w_ada"][0].rearrange("(k p) n -> p k n", p=P)
        block = ctx.enter_context(nc.Block())

        @block.sync
        def _(sp):
            sp.dma_start(c9[0:1, :], a["c_prompt"]).then_inc(s["c_in"], 16)
            sp.dma_start(c9[1:NC, :], a["c_sample"]).then_inc(s["c_in"], 16)
            with sp.Fori(0, NP // BUF) as i:
                for j in range(BUF):
                    sp.wait_ge(s[f"w_free{j}"], i + 1)
                    sp.wait_ge(s[f"mod_free{j}"], i + 1)
                    cols = bass.ds((i * BUF + j) * 512, 512)
                    sp.dma_start(wada[j][:, :, :], w_view[:, :, cols]).then_inc(s[f"w_in{j}"], 16)
                    sp.dma_start(bada[j][:, :], a["b_ada"][0:1, cols].broadcast_to([NC, 512])).then_inc(s[f"b_in{j}"], 16)

        @block.gpsimd
        def _(pool):
            pool.memset(ident[:, :], 0.0).then_inc(s["ident0"], 1)
            pool.wait_ge(s["ident0"], 1)
            pool.affine_select(out=ident[:, :], in_=ident[:, :], compare_op=ALU.not_equal, fill=1.0,
                               base=0, pattern=[[-1, P]], channel_multiplier=1).then_inc(s["ident"], 1)
            pool.memset(blank[:, :, 0], 0)
            pool.iota(blank[:, :, 1], [[1, SLOTS // P]], base=NT * TOPK, channel_multiplier=SLOTS // P).then_inc(s["blank"], 1)
            pool.wait_ge(s["blank"], 1)
            pool.dma_start(scratch["slots"].rearrange("(p n) c -> p n c", p=P), blank[:, :, :]).then_inc(s["list_out"], 16)
            pool.wait_ge(s["list_out"], 16)

        @block.tensor
        def _(pe):
            for j in range(BUF):
                pe.sem_inc(s[f"w_free{j}"], 1)
            pe.wait_ge(s["ident"], 1)
            pe.wait_ge(s["c_silu"], 1)
            for k in range(KT):
                last = pe.transpose(pt[:, k * NC:(k + 1) * NC], sig[:, k * P:(k + 1) * P], ident[0:NC, 0:NC])
            last.then_inc(s["cT_ps"], 1)
            pe.wait_ge(s["cT"], 1)
            with pe.Fori(0, NP // BUF) as i:
                for j in range(BUF):
                    pe.wait_ge(s[f"w_in{j}"], i * 16 + 16)
                    pe.wait_ge(s[f"mod_free{j}"], i + 1)
                    for k in range(KT):
                        last = pe.matmul(pm[j][0:NC, :], cT[:, k * NC:(k + 1) * NC], wada[j][:, k, :],
                                         start=(k == 0), stop=(k == KT - 1))
                    last.then_inc(s[f"w_free{j}"], 1)

        @block.scalar
        def _(act):
            act.wait_ge(s["c_in"], 32)
            act.activation(sig[:, :], c9[:, :], ACT.Sigmoid).then_inc(s["c_sig"], 1)
            with act.Fori(0, NP // BUF) as i:
                for j in range(BUF):
                    act.wait_ge(s[f"mod{j}"], i + 1)
                    act.dma_start(scratch["mod"][:, bass.ds((i * BUF + j) * 512, 512)], modt[j][:, :]).then_inc(s[f"mod_out{j}"], 16)
            for j in range(BUF):
                act.wait_ge(s[f"mod_out{j}"], 16 * (NP // BUF) + 16)

        @block.vector
        def _(dve):
            for j in range(BUF):
                dve.sem_inc(s[f"mod_free{j}"], 1)
                dve.sem_inc(s[f"mod_out{j}"], 16)
            dve.wait_ge(s["c_sig"], 1)
            dve.tensor_tensor(sig[:, :], sig[:, :], c9[:, :], ALU.mult).then_inc(s["c_silu"], 1)
            dve.wait_ge(s["cT_ps"], 1)
            dve.tensor_copy(cT[:, :], pt[:, 0:KT * NC]).then_inc(s["cT"], 1)
            with dve.Fori(0, NP // BUF) as i:
                for j in range(BUF):
                    dve.wait_ge(s[f"w_free{j}"], i + 2)
                    dve.wait_ge(s[f"b_in{j}"], i * 16 + 16)
                    dve.wait_ge(s[f"mod_out{j}"], i * 16 + 16)
                    dve.tensor_tensor(modt[j][:, :], pm[j][0:NC, :], bada[j][:, :], ALU.add).then_inc(s[f"mod{j}"], 1)
                    dve.engine_nop().then_inc(s[f"mod_free{j}"], 1)
    s.clear()


def mixing(nc, a, scratch, out, keep):
    s = Signals(nc, "mix")
    with ExitStack() as ctx:
        def sb(name, shape, dt=F32):
            return ctx.enter_context(nc.sbuf_tensor(name, shape, dt))

        probs, pdense = keep["probs"], keep["pdense"]
        ident = keep["ident"]
        w_in = sb("w_in", [P, KT, D_IN])
        w_out = sb("w_out", [P, KT, D])
        w_pool = sb("w_pool", [P, H, P])
        w_rt = sb("w_rt", [P, KT, E])
        mul1, add1, gate1, mul2, add2 = (sb(n, [P, D]) for n in ("mul1", "add1", "gate1", "mul2", "add2"))
        hnorm = sb("hnorm", [P, HW])
        b_rt = sb("b_rt", [P, E])
        small = sb("small", [3 * H, P])
        cols = sb("cols", [P, 3 * H])
        lbd = sb("lbd", [P, H])
        lb = sb("lb", [P, H])
        oml = sb("oml", [P, H])
        eps = sb("eps", [P, 1])
        ones = sb("ones", [P, P])
        tri = sb("tri", [P, P])
        masks = [sb(f"mask{i}", [P, P]) for i in range(len(BLOCKS))]
        reset = sb("reset", [P, HW])
        reset_s = sb("reset_s", [P, H * NS])
        seqmask = sb("seqmask", [NS, NB])
        iota_e = sb("iota_e", [P, E])
        iota_i = sb("iota_i", [P, E], I32)
        entries = sb("entries", [P, TILES + 1, TOPK, 2], I32)
        slot0 = sb("slot0", [P, E])
        icnt = sb("icnt", [P, H, P])
        x = sb("x", [P, D])
        h = sb("h", [P, D])
        hT = sb("hT", [P, KT * P])
        f, q, k, lf, b, eb, qb, kend, dk = (sb(n, [P, HW]) for n in ("f", "q", "k", "lf", "b", "eb", "qb", "kend", "dk"))
        sgf, sgq = f, q
        v, gs = sb("v", [P, HW]), sb("gs", [P, HW])
        lev = [sb(f"lev{i}", [P, HW]) for i in range(2)]
        A = sb("A", [P, HW])
        S = sb("S", [P, HW])
        kT = dk
        o = kend
        wd = b
        vx = sb("vx", [P, H, HIST + P])
        pw1 = sb("pw1", [P, 5 * P])
        pw2 = sb("pw2", [P, 5 * P])
        mixT = sb("mixT", [P, KT * P])
        ss = sb("ss", [P, 8])
        rs = sb("rs", [P, 8])
        lg = sb("lg", [P, E])
        top = sb("top", [P, 8])
        topi = sb("topi", [P, 8], U32)
        topf = sb("topf", [P, 8])
        sm = sb("sm", [P, 16])
        hot = sb("hot", [P, TOPK * E])
        hotp = sb("hotp", [P, TOPK * E])
        chosen = sb("chosen", [P, E])
        pos = sb("pos", [P, E])
        slotf = sb("slotf", [P, TOPK])
        slotc = sb("slotc", [P, TOPK], I32)
        entry = sb("entry", [P, TOPK, 2], I32)
        im = {n: sb("im_" + n, [P, E]) for n in ("m", "t", "cum", "le", "lem", "hot")}
        ic = sb("ic", [P, 16])
        tab_f = sb("tab_f", [ITEMS + 1, 3], I32)
        region0 = sb("region0", [P, E])
        iota_pi = sb("iota_pi", [P, 1], I32)
        iota_p = sb("iota_p", [P, 1])
        ramp = sb("ramp", [P, P], I32)
        junk = mixT

        pA, pB, pQ, pF, pV, pI, pG, pW = (ctx.enter_context(nc.psum_tensor(n, [P, 512], F32))
                                          for n in ("pA", "pB", "pQ", "pF", "pV", "pI", "pG", "pW"))
        flat_in = w_in[:, :, :].rearrange("p k n -> p (k n)")
        NBH = NB * H
        S0 = flat_in[:, 0:NBH * P].rearrange("p (b h v) -> p b h v", b=NB, h=H)
        Vz = flat_in[0:NS, NBH * P:2 * NBH * P].rearrange("p (b n) -> p b n", b=NB)
        Qz = flat_in[:, 2 * NBH * P:2 * NBH * P + H * NB * NS]
        hist = flat_in[0:NB * HIST, 3 * NBH * P:3 * NBH * P + HW]
        rest = 3 * NBH * P + HW
        vxs = flat_in[:, rest:rest + H * NB * (HIST + TS)].rearrange("p (h b t) -> p h b t", h=H, b=NB)
        rest += H * NB * (HIST + TS)
        vtc = flat_in[:, rest:rest + H * NS]
        lvl_ps = (pQ, pF)

        block = ctx.enter_context(nc.Block())
        mod = scratch["mod"]
        adds = ((mul1, SC1), (add1, SH1), (gate1, G1), (mul2, SC2), (add2, SH2))

        @block.sync
        def _(sp):
            sp.dma_start(small[0:2 * H, :], a["lower_bounds"].rearrange("r (h p) -> (r h) p", p=P)).then_inc(s["small_in"], 16)
            sp.dma_start(small[2 * H:3 * H, :], a["pool_scale"].rearrange("o (h p) -> (o h) p", p=P)).then_inc(s["small_in"], 16)
            sp.dma_start(x[:, :], a["norm1"].broadcast_to([P, D])).then_inc(s["rows_in"], 16)
            sp.dma_start(h[:, :], a["norm2"].broadcast_to([P, D])).then_inc(s["rows_in"], 16)
            for dst, m in adds:
                sp.dma_start(dst[:, :], mod[0:1, m * D:(m + 1) * D].broadcast_to([P, D])).then_inc(s["rows_in"], 16)
            sp.dma_start(hnorm[:, :], a["hgrn_norm"].rearrange("o h p -> o (h p)").broadcast_to([P, HW])).then_inc(s["rows_in"], 16)
            sp.dma_start(b_rt[:, :], a["b_router"].broadcast_to([P, E])).then_inc(s["rows_in"], 16)
            for j in (1, 0, 4, 2, 3):
                sp.dma_start(w_in[:, :, j * HW:(j + 1) * HW],
                             a["w_in"][0].rearrange("(k p) n -> p k n", p=P)[:, :, j * HW:(j + 1) * HW]).then_inc(s[f"w_in{j}"], 16)
                if j == 1:
                    sp.wait_ge(s["x_free"], 1)
                    sp.dma_start(x[:, :], a["x_prompt"][0, 0:P, :]).then_inc(s["x_in"], 16)
            sp.dma_start(w_out[:, :, :], a["w_out"][0].rearrange("(k p) n -> p k n", p=P)).then_inc(s["w_out"], 16)
            sp.dma_start(w_pool[:, :, :], a["w_pool"][0].rearrange("g c d -> c g d")).then_inc(s["w_pool"], 16)
            sp.dma_start(w_rt[:, :, :], a["w_router"][0].rearrange("(k p) n -> p k n", p=P)).then_inc(s["w_rt"], 16)

            def store(t):
                sp.wait_ge(s["x1"], t + 1)
                sp.dma_start(scratch["x1"][bass.ds(t * P, P), :], x[:, :]).then_inc(s["x1_out"], 16)
                sp.wait_ge(s["h2"], 2 * t + 2)
                sp.dma_start(scratch["h2"][bass.ds(t * P, P), :], h[:, :]).then_inc(s["h2_out"], 16)
                sp.wait_ge(s["x1_out"], t * 16 + 16)
                sp.sem_inc(s["met"], 1)

            with sp.Fori(0, TILES - 1) as t:
                store(t)
                sp.dma_start(x[:, :], a["x_prompt"][0, bass.ds(t * P + P, P), :]).then_inc(s["x_in"], 16)
            store(TILES - 1)
            sp.wait_ge(s["S"], TILES + 1)
            sp.dma_start(out["S_p"][0, 0].rearrange("h k v -> k h v"), S[:, :].rearrange("p (h v) -> p h v", h=H)).then_inc(s["st_out"], 16)
            sp.wait_ge(s["h2_out"], 16 * (TILES + 1))
            sp.wait_ge(s["h2T_ps"], 2 * TILES)
            sp.dma_start(x[0:NS, :], a["norm1"].broadcast_to([NS, D])).then_inc(s["rows_s"], 16)
            sp.dma_start(h[0:NS, :], a["norm2"].broadcast_to([NS, D])).then_inc(s["rows_s"], 16)
            for dst, m in adds:
                for j in range(NB):
                    sp.dma_start(dst[j * TS:(j + 1) * TS, :], mod[1 + j:2 + j, m * D:(m + 1) * D].broadcast_to([TS, D])).then_inc(s["rows_s"], 16)
            sp.wait_ge(s["rows_s_set"], 1)
            sp.dma_start(x[0:NS, :], a["x_sample"].rearrange("b t d -> (b t) d")).then_inc(s["x_in"], 16)
            sp.wait_ge(s["g_mm"], TILES + 1)
            sp.dma_start(S0, a["state_hgrn"][0].rearrange("b h k v -> k b h v")).then_inc(s["s0_in"], 16)
            sp.dma_start(hist, a["state_pool"][0].rearrange("b r c -> (b r) c")).then_inc(s["hist_in"], 16)
            sp.dma_start(out["H_s"][0, :, 0:HIST - TS, :], a["state_pool"][0, :, TS:HIST, :]).then_inc(s["st_out"], 16)
            sp.wait_ge(s["x1"], TILES + 1)
            sp.dma_start(scratch["x1"][NTOK:NT, :], x[0:NS, :]).then_inc(s["x1_out"], 16)
            sp.wait_ge(s["h2"], 2 * TILES + 2)
            sp.dma_start(scratch["h2"][NTOK:NT, :], h[0:NS, :]).then_inc(s["h2_out"], 16)
            sp.wait_ge(s["S_s"], NBH)
            sp.dma_start(out["S_s"][0].rearrange("b h k v -> k b h v"), S0).then_inc(s["st_out"], 16)
            sp.wait_ge(s["items"], 1)
            sp.dma_start(scratch["table"], tab_f[:, :]).then_inc(s["tab_out"], 16)
            sp.wait_ge(s["tab_out"], 16)
            sp.wait_ge(s["st_out"], 16 * 3)
            sp.wait_ge(s["x1_out"], 16 * (TILES + 1))
            sp.wait_ge(s["h2_out"], 16 * (TILES + 2))

        def pe_route(pe, t, T):
            done = t + 1
            pe.wait_ge(s["chosen"], done)
            pe.matmul(pB[0:T, 0:E], tri[0:T, 0:T], chosen[0:T, :], start=True, stop=True)
            pe.matmul(pB[:, E:2 * E], ones[0:T, :], chosen[0:T, :], start=True, stop=True).then_inc(s["rank_mm"], 1)

        def pe_tile(pe, t, T, G, blocks, sample):
            done = t + 1

            def pooling():
                pe.wait_ge(s["w_pool"], 16)
                pe.wait_ge(s["pool_d"], done)
                for m in range(H):
                    last = pe.matmul(pV[:, m * T:(m + 1) * T], w_pool[:, m, :], pw1[:, m * T:(m + 1) * T], start=True, stop=True)
                last.then_inc(s["pool_mm"], 1)

            for half, bank in enumerate((pA, pB)):
                pe.wait_ge(s["h1"], 2 * t + half + 1)
                for c in range(4):
                    kt = half * 4 + c
                    last = pe.transpose(bank[:, c * T:(c + 1) * T], h[0:T, kt * P:(kt + 1) * P], ident[0:T, 0:T])
                last.then_inc(s["hT_ps"], 1)
            pe.wait_ge(s["hT_lo"], done)
            pe.wait_ge(s["hT_hi"], done)

            for bank, first, name in ((pF, HW, "f_mm"), (pQ, 0, "q_mm"), (pV, 4 * HW, "v_mm")):
                pe.wait_ge(s[f"w_in{first // HW}"], 16)
                for m in range(H):
                    for kt in range(KT):
                        last = pe.matmul(bank[:, m * T:(m + 1) * T], w_in[:, kt, first + m * P:first + (m + 1) * P],
                                         hT[:, kt * T:(kt + 1) * T], start=(kt == 0), stop=(kt == KT - 1))
                last.then_inc(s[name], 1)
                if name == "f_mm" and not first_tile(t):
                    pe_route(pe, t - 1, P)
            if not first_tile(t):
                pe.wait_ge(s["lg"], t)
            for bank, first, name in ((pI, 2 * HW, "i_mm"), (pG, 3 * HW, "g_mm")):
                pe.wait_ge(s[f"w_in{first // HW}"], 16)
                for kt in range(KT):
                    last = pe.matmul(bank[0:T, :], hT[:, kt * T:(kt + 1) * T], w_in[:, kt, first:first + HW],
                                     start=(kt == 0), stop=(kt == KT - 1))
                last.then_inc(s[name], 1)

            if sample:
                pe.wait_ge(s["hist_in"], 16)
                pe.wait_ge(s["rank_used"], TILES)
                for m in range(H):
                    last = pe.transpose(pB[:, m * NB * HIST:(m + 1) * NB * HIST], hist[:, m * P:(m + 1) * P], ident[0:NB * HIST, 0:NB * HIST])
                last.then_inc(s["hist_ps"], 1)
                pe.wait_ge(s["vtc"], 1)
                for m in range(H):
                    last = pe.transpose(pA[0:NS, m * P:(m + 1) * P], vtc[:, m * NS:(m + 1) * NS], ident[:, :])
                last.then_inc(s["vrow_s_ps"], 1)
                pe.wait_ge(s["vrow_s"], 1)

            pe.wait_ge(s["k"], done)
            pe.wait_ge(s["q"], done)
            for m in range(H):
                last = pe.matmul(pQ[0:T, m * T:(m + 1) * T], k[:, m * T:(m + 1) * T], q[:, m * T:(m + 1) * T],
                                 start=True, stop=True)
            last.then_inc(s["lvl_mm"], 1)
            base, level = t * LV, t * (LV - 1)
            for i in range(len(blocks)):
                pe.wait_ge(s["lev"], level + i + 1)
                if i >= 1:
                    pe.wait_ge(s["lvl"], base + i)
                xl = lev[i % 2]
                for m in range(H):
                    last = pe.matmul(lvl_ps[(i + 1) % 2][0:T, m * T:(m + 1) * T], xl[:, m * T:(m + 1) * T],
                                     xl[:, m * T:(m + 1) * T], start=True, stop=True)
                last.then_inc(s["lvl_mm"], 1)

            pe.wait_ge(s["kend"], done)
            for m in range(H):
                last = pe.transpose(pW[0:T, m * P:(m + 1) * P], kend[:, m * T:(m + 1) * T], ident[:, :])
            last.then_inc(s["kT_ps"], 1)

            if sample:
                pooling()

            pe.wait_ge(s["v"], done)
            pe.wait_ge(s["qb"], done)
            pe.wait_ge(s["lvl"], base + len(blocks) + 1)
            if not sample:
                pe.wait_ge(s["S"], done)
                for m in range(H):
                    pe.matmul(pI[0:T, m * P:(m + 1) * P], qb[:, m * T:(m + 1) * T], S[:, m * P:(m + 1) * P], start=True, stop=False)
                    last = pe.matmul(pI[0:T, m * P:(m + 1) * P], A[0:T, m * T:(m + 1) * T], v[0:T, m * P:(m + 1) * P], start=False, stop=True)
                last.then_inc(s["o_mm"], 1)
                pe.wait_ge(s["kT"], done)
                pe.wait_ge(s["gs"], done)
                for m in range(H):
                    last = pe.matmul(pG[:, m * P:(m + 1) * P], kT[0:T, m * P:(m + 1) * P], v[0:T, m * P:(m + 1) * P], start=True, stop=True)
                last.then_inc(s["S_mm"], 1)
            else:
                pe.wait_ge(s["Qz"], 1)
                pe.wait_ge(s["s0_in"], 16)
                for m in range(H):
                    for j in range(NB):
                        pe.matmul(pI[0:T, m * P:(m + 1) * P], Qz[:, (m * NB + j) * NS:(m * NB + j + 1) * NS], S0[:, j, m, :],
                                  start=(j == 0), stop=False)
                    last = pe.matmul(pI[0:T, m * P:(m + 1) * P], A[0:T, m * T:(m + 1) * T], v[0:T, m * P:(m + 1) * P], start=False, stop=True)
                last.then_inc(s["o_mm"], 1)
                pe.wait_ge(s["kT"], done)
                pe.wait_ge(s["Vz"], 1)
                pe.wait_ge(s["gs"], done)
                for j in range(NB):
                    bank = (pG, pF)[j % 2]
                    if j >= 2:
                        pe.wait_ge(s["S_s"], H * (j - 1))
                    for m in range(H):
                        last = pe.matmul(bank[:, m * P:(m + 1) * P], kT[0:T, m * P:(m + 1) * P], Vz[:, j, m * P:(m + 1) * P], start=True, stop=True)
                    last.then_inc(s["S_s_mm"], 1)

            if not sample:
                pooling()

            pe.wait_ge(s["o"], done)
            for m in range(H):
                last = pe.transpose(pA[:, m * T:(m + 1) * T], o[0:T, m * P:(m + 1) * P], ident[0:T, 0:T])
            last.then_inc(s["oT_ps"], 1)
            pe.wait_ge(s["oT"], done)
            pe.wait_ge(s["pool_y"], done)
            pe.wait_ge(s["w_out"], 16)
            for n, bank in enumerate((pW, pQ)):
                for kt in range(KT):
                    last = pe.matmul(bank[0:T, :], mixT[:, kt * T:(kt + 1) * T], w_out[:, kt, n * 512:(n + 1) * 512],
                                     start=(kt == 0), stop=(kt == KT - 1))
                last.then_inc(s["out_mm"], 1)

            if not first_tile(t):
                pe.wait_ge(s["rank_used"], t)
            for half, bank in enumerate((pA, pB)):
                pe.wait_ge(s["h2"], 2 * t + half + 1)
                for c in range(4):
                    kt = half * 4 + c
                    last = pe.transpose(bank[:, c * T:(c + 1) * T], h[0:T, kt * P:(kt + 1) * P], ident[0:T, 0:T])
                last.then_inc(s["h2T_ps"], 1)
            pe.wait_ge(s["h2T_lo"], done)
            pe.wait_ge(s["h2T_hi"], done)
            pe.wait_ge(s["w_rt"], 16)
            for kt in range(KT):
                last = pe.matmul(pI[0:T, 0:E], hT[:, kt * T:(kt + 1) * T], w_rt[:, kt, :], start=(kt == 0), stop=(kt == KT - 1))
            last.then_inc(s["router_mm"], 1)

        LV = len(BLOCKS) + 1

        @block.tensor
        def _(pe):
            pe.wait_ge(s["consts"], 1)
            pe.wait_ge(s["small_in"], 32)
            pe.transpose(pA[:, 0:3 * H], small[:, :], ident[0:3 * H, 0:3 * H]).then_inc(s["cols_ps"], 1)
            pe.wait_ge(s["cols"], 1)
            pe_tile(pe, 0, P, P, BLOCKS, False)
            with pe.Fori(1, TILES) as t:
                pe_tile(pe, t, P, P, BLOCKS, False)
            pe.wait_ge(s["rank_used"], TILES - 1)
            for m in range(H):
                last = pe.transpose(pB[:, m * P:(m + 1) * P], vx[:, m, HIST:HIST + P], ident[:, :])
            last.then_inc(s["vrow_ps"], 1)
            pe.wait_ge(s["vrow"], 1)
            pe_tile(pe, TILES, NS, TS, BLOCKS_S, True)
            pe_route(pe, TILES, NS)

        def act_norm(act, src, T, col, done, tag):
            act.activation(junk[0:T, :], src, ACT.Square,
                           accum_out=ss[0:T, col:col + 1]).then_inc(s["ss" + tag], 1)
            act.wait_ge(s["ss" + tag], done)
            act.activation(rs[0:T, col:col + 1], ss[0:T, col:col + 1], ACT.Sqrt, scale=1.0 / D, bias=eps[0:T, :]).then_inc(s["root" + tag], 1)

        def act_route(act, t, T):
            done = t + 1
            act.wait_ge(s["nmax"], done)
            act.activation(sm[0:T, 1:5], top[0:T, 0:TOPK], ACT.Exp, bias=sm[0:T, 0:1], accum_out=sm[0:T, 5:6]).then_inc(s["etop"], 1)

        def act_tile(act, t, T, G, blocks, sample):
            done = t + 1
            n = H * T

            def decays():
                act.wait_ge(s["f"], done)
                act.activation(lf[:, 0:n], f[:, 0:n], ACT.Ln).then_inc(s["lf"], 1)
                act.wait_ge(s["b"], done)
                act.activation(eb[:, 0:n], b[:, 0:n], ACT.Exp).then_inc(s["eb"], 1)
                act.wait_ge(s["dk"], done)
                act.activation(dk[:, 0:n], dk[:, 0:n], ACT.Exp).then_inc(s["ek"], 1)

            def gates():
                act.wait_ge(s["g_mm"], done)
                act.activation(gs[0:T, :], pG[0:T, :], ACT.Sigmoid).then_inc(s["sgg"], 1)

            act.wait_ge(s["x_in"], 16 * done if isinstance(t, int) else t * 16 + 16)
            act_norm(act, x[0:T, :], T, 0, done, "1")
            act.wait_ge(s["hT_ps"], 2 * t + 1)
            act.activation(hT[:, 0:4 * T], pA[:, 0:4 * T], ACT.Copy).then_inc(s["hT_lo"], 1)
            if not first_tile(t):
                act_route(act, t - 1, P)
            act.wait_ge(s["f_mm"], done)
            act.activation(sgf[:, 0:n], pF[:, 0:n], ACT.Sigmoid).then_inc(s["sgf"], 1)
            act.wait_ge(s["q_mm"], done)
            act.activation(sgq[:, 0:n], pQ[:, 0:n], ACT.Sigmoid).then_inc(s["sgq"], 1)
            if not sample:
                decays()
            act.wait_ge(s["v_mm"], done)
            if not sample:
                act.wait_ge(s["carried"], done)
                act.activation(vx[:, :, HIST:HIST + T], pV[:, 0:n].rearrange("p (h t) -> p h t", h=H), ACT.Copy).then_inc(s["vx"], 1)
            act.wait_ge(s["i_mm"], done)
            act.activation(v[0:T, :], pI[0:T, :], ACT.Copy).then_inc(s["v"], 1)
            if sample:
                gates()
                act.activation(vtc, pV[:, 0:n], ACT.Copy).then_inc(s["vtc"], 1)
                act.activation(vxs[:, :, :, HIST:HIST + TS], pV[:, 0:n].rearrange("p (h b t) -> p h b t", h=H, b=NB), ACT.Copy)
                act.wait_ge(s["hist_ps"], 1)
                act.activation(vxs[:, :, :, 0:HIST], pB[:, 0:H * NB * HIST].rearrange("p (h b t) -> p h b t", h=H, b=NB), ACT.Copy).then_inc(s["vx"], 1)
                act.wait_ge(s["vrow_s_ps"], 1)
                act.activation(junk[0:NS, 0:HW], pA[0:NS, :], ACT.Copy).then_inc(s["vrow_s"], 1)
                act.wait_ge(s["vrow_s"], 1)
                for j in range(NB):
                    act.dma_start(out["H_s"][0, j, HIST - TS:HIST, :], junk[j * TS:(j + 1) * TS, 0:HW]).then_inc(s["vrow_out"], 16)
                act.wait_ge(s["vrow_out"], 16 + 16 * NB)
            if sample:
                decays()
            level = t * (LV - 1)
            for i in range(len(blocks)):
                act.wait_ge(s["dlev"], level + i + 1)
                act.activation(lev[i % 2][:, 0:n], lev[i % 2][:, 0:n], ACT.Exp).then_inc(s["elev"], 1)
            act.wait_ge(s["kT_ps"], done)
            act.activation(kT[0:T, :], pW[0:T, :], ACT.Copy).then_inc(s["kT"], 1)
            if not sample:
                gates()
            act.wait_ge(s["o_mm"], done)
            for m in range(H):
                last = act.activation(junk[0:T, m * P:(m + 1) * P], pI[0:T, m * P:(m + 1) * P], ACT.Square,
                                      accum_out=ss[0:T, 2 + m:3 + m])
            last.then_inc(s["sso"], 1)
            act.wait_ge(s["sso"], done)
            act.activation(rs[0:T, 2:2 + H], ss[0:T, 2:2 + H], ACT.Sqrt, scale=1.0 / P, bias=eps[0:T, :]).then_inc(s["rooto"], 1)
            act.wait_ge(s["oT_ps"], done)
            act.activation(mixT[:, 0:n], pA[:, 0:n], ACT.Copy).then_inc(s["oT"], 1)
            act.wait_ge(s["x1"], done)
            act_norm(act, x[0:T, :], T, 1, done, "2")
            act.wait_ge(s["h2T_ps"], 2 * t + 1)
            act.activation(hT[:, 0:4 * T], pA[:, 0:4 * T], ACT.Copy).then_inc(s["h2T_lo"], 1)

        @block.scalar
        def _(act):
            act.wait_ge(s["lbd"], 1)
            act.activation(lb[:, :], lbd[:, :], ACT.Sigmoid).then_inc(s["lb"], 1)
            act.wait_ge(s["consts"], 1)
            act_tile(act, 0, P, P, BLOCKS, False)
            with act.Fori(1, TILES) as t:
                act_tile(act, t, P, P, BLOCKS, False)
            act.wait_ge(s["vrow_ps"], 1)
            act.activation(junk[:, 0:HW], pB[:, :], ACT.Copy).then_inc(s["vrow"], 1)
            act.wait_ge(s["vrow"], 1)
            act.dma_start(out["H_p"][0, 0], junk[P - HIST:P, 0:HW]).then_inc(s["vrow_out"], 16)
            act.wait_ge(s["vrow_out"], 16)
            act_tile(act, TILES, NS, TS, BLOCKS_S, True)
            act_route(act, TILES, NS)

        def halves(ap, B):
            w = ap.rearrange("p (j two c) -> p j two c", two=2, c=B)
            return w[:, :, 0, :], w[:, :, 1, :], w[:, :, 0, B - 1:B]

        def dve_norm(dve, T, c, n, tag, done):
            dve.wait_ge(s["root" + tag], done)
            dve.reciprocal(rs[0:T, c:c + n], rs[0:T, c:c + n]).then_inc(s["r" + tag], 1)

        def dve_route(dve, t, T):
            done = t + 1
            dve.wait_ge(s["router_mm"], done)
            dve.tensor_tensor(lg[0:T, :], pI[0:T, 0:E], b_rt[0:T, :], ALU.add).then_inc(s["lg"], 1)
            dve.wait_ge(s["lg"], done)
            dve.sem_inc(s["met"], 1)
            dve.max(top[0:T, :], lg[0:T, :]).then_inc(s["top"], 1)
            dve.wait_ge(s["top"], done)
            dve.tensor_scalar(sm[0:T, 0:1], top[0:T, 0:1], -1.0, None, ALU.mult).then_inc(s["nmax"], 1)
            dve.max_index(topi[0:T, :], top[0:T, :], lg[0:T, :]).then_inc(s["topi"], 1)
            dve.wait_ge(s["topi"], done)
            dve.tensor_copy(topf[0:T, :], topi[0:T, :]).then_inc(s["topf"], 1)
            dve.wait_ge(s["etop"], done)
            dve.reciprocal(sm[0:T, 6:7], sm[0:T, 5:6]).then_inc(s["rsum"], 1)
            dve.wait_ge(s["rsum"], done)
            pr = probs[0:T, bass.ds(t, 1), :] if not isinstance(t, int) else probs[0:T, t:t + 1, :]
            dve.tensor_scalar(sm[0:T, 8:12], sm[0:T, 1:5], sm[0:T, 6:7], None, ALU.mult).then_inc(s["prob"], 1)
            dve.wait_ge(s["topf"], done)
            dve.wait_ge(s["prob"], done)
            dve.tensor_copy(pr, sm[0:T, 8:12].unsqueeze(1))
            for c in range(TOPK):
                dve.tensor_scalar(hot[0:T, c * E:(c + 1) * E], iota_e[0:T, :], topf[0:T, c:c + 1], None, ALU.is_equal)
                last = dve.tensor_scalar(hotp[0:T, c * E:(c + 1) * E], iota_e[0:T, :], topf[0:T, c:c + 1], sm[0:T, 8 + c:9 + c], ALU.is_equal, ALU.mult)
            last.then_inc(s["hot"], 1)
            dve.wait_ge(s["hot"], done)
            dve.tensor_reduce(chosen[0:T, :], hot[0:T, :].rearrange("p (c e) -> p e c", c=TOPK), AX, ALU.add).then_inc(s["chosen"], 1)
            pd = pdense[0:T, bass.ds(t, 1), :] if not isinstance(t, int) else pdense[0:T, t:t + 1, :]
            dve.tensor_reduce(pos[0:T, :], hotp[0:T, :].rearrange("p (c e) -> p e c", c=TOPK), AX, ALU.add).then_inc(s["pd"], 1)
            dve.wait_ge(s["pd"], done)
            dve.tensor_copy(pd, pos[0:T, :].unsqueeze(1)).then_inc(s["pd_kept"], 1)
            dve.wait_ge(s["rank_mm"], done)
            dve.wait_ge(s["pd_kept"], done)
            dve.tensor_tensor(pos[0:T, :], pB[0:T, 0:E], slot0[0:T, :], ALU.add).then_inc(s["pos"], 1)
            dve.wait_ge(s["pos"], done)
            dve.tensor_tensor(hot[0:T, :].rearrange("p (c e) -> p c e", c=TOPK), hot[0:T, :].rearrange("p (c e) -> p c e", c=TOPK),
                              pos[0:T, :].unsqueeze(1).broadcast_to([T, TOPK, E]), ALU.mult).then_inc(s["hotpos"], 1)
            dve.tensor_tensor(slot0[:, :], slot0[:, :], pB[:, E:2 * E], ALU.add).then_inc(s["rank_used"], 1)
            dve.wait_ge(s["hotpos"], done)
            dve.tensor_reduce(slotf[0:T, :], hot[0:T, :].rearrange("p (c e) -> p c e", c=TOPK), AX, ALU.add).then_inc(s["slotf"], 1)
            dve.wait_ge(s["slotf"], done)
            dve.wait_ge(s["slotc_free"], done)
            en = entries[:, bass.ds(t, 1)] if not isinstance(t, int) else entries[:, t:t + 1]
            dve.tensor_copy(entry[:, :, :].rearrange("p c w -> p (c w)"), en.rearrange("p o c w -> p (o c w)"))
            dve.tensor_copy(slotc[0:T, :], slotf[0:T, :]).then_inc(s["slotc"], 1)

        def dve_tile(dve, t, T, G, blocks, sample):
            done = t + 1
            n = H * T

            def gates():
                dve.wait_ge(s["sgg"], done)
                dve.tensor_tensor(gs[0:T, :], gs[0:T, :], pG[0:T, :], ALU.mult).then_inc(s["gs"], 1)

            dve_norm(dve, T, 0, 1, "1", done)
            dve.wait_ge(s["r1"], done)
            if not sample:
                dve.wait_ge(s["h2_out"], t * 16 + 16)
            for half in range(2):
                cut = slice(half * 512, (half + 1) * 512)
                dve.scalar_tensor_tensor(out=h[0:T, cut], in0=x[0:T, cut], scalar=rs[0:T, 0:1], in1=mul1[0:T, cut], op0=ALU.mult, op1=ALU.mult).then_inc(s["h0"], 1)
                dve.wait_ge(s["h0"], 2 * t + half + 1)
                dve.tensor_tensor(h[0:T, cut], h[0:T, cut], add1[0:T, cut], ALU.add).then_inc(s["h1"], 1)
            dve.wait_ge(s["hT_ps"], 2 * t + 2)
            dve.tensor_copy(hT[:, 4 * T:8 * T], pB[:, 0:4 * T]).then_inc(s["hT_hi"], 1)
            if not first_tile(t):
                dve_route(dve, t - 1, P)
            dve.wait_ge(s["sgf"], done)
            for m in range(H):
                last = dve.tensor_scalar(f[:, m * T:(m + 1) * T], sgf[:, m * T:(m + 1) * T], oml[:, m:m + 1], lb[:, m:m + 1], ALU.mult, ALU.add)
            last.then_inc(s["f"], 1)
            dve.wait_ge(s["sgq"], done)
            dve.tensor_tensor(q[:, 0:n], sgq[:, 0:n], pQ[:, 0:n], ALU.mult).then_inc(s["q"], 1)
            dve.wait_ge(s["lf"], done)
            rmask = reset_s if sample else reset
            dve.tensor_tensor_scan(b[:, 0:n], rmask[:, 0:n], lf[:, 0:n], 0.0, ALU.mult, ALU.add).then_inc(s["b"], 1)
            dve.wait_ge(s["b"], done)
            bg = b[:, 0:n].rearrange("p (g c) -> p g c", c=G)
            dve.tensor_tensor(dk[:, 0:n].rearrange("p (g c) -> p g c", c=G), bg[:, :, G - 1:G].broadcast_to([P, n // G, G]), bg, ALU.subtract).then_inc(s["dk"], 1)
            if sample:
                gates()

            base = t * LV

            def take(i):
                dve.wait_ge(s["lvl_mm"], base + i + 1)
                if i:
                    dve.wait_ge(s["lvl"], base + i)
                dve.sem_inc(s["met"], 1)
                mask = ident if i == 0 else masks[i - 1]
                dve.copy_predicated(A[0:T, 0:n].rearrange("p (h t) -> p h t", h=H),
                                    mask[0:T, 0:T].bitcast(I32).unsqueeze(1).broadcast_to([T, H, T]),
                                    (pQ if i == 0 else lvl_ps[i % 2])[0:T, 0:n].rearrange("p (h t) -> p h t", h=H)).then_inc(s["lvl"], 1)

            for i, B in enumerate(blocks):
                if i >= 2:
                    dve.wait_ge(s["lvl_mm"], base + i)
                left, right, border = halves(b[:, 0:n], B)
                dl, dr, _ = halves(lev[i % 2][:, 0:n], B)
                dve.tensor_tensor(dl, border.broadcast_to(list(left.shape)), left, ALU.subtract)
                dve.tensor_tensor(dr, right, border.broadcast_to(list(left.shape)), ALU.subtract).then_inc(s["dlev"], 1)
                if i == 1:
                    take(0)
                if i >= 2:
                    take(i - 1)
            take(len(blocks) - 1)
            take(len(blocks))

            if not sample:
                gates()
                dve.wait_ge(s["S_mm"], done)
                for m in range(H):
                    last = dve.scalar_tensor_tensor(out=S[:, m * P:(m + 1) * P], in0=S[:, m * P:(m + 1) * P], scalar=eb[:, (m + 1) * T - 1:(m + 1) * T],
                                                    in1=pG[:, m * P:(m + 1) * P], op0=ALU.mult, op1=ALU.add)
                last.then_inc(s["S"], 1)
            dve_norm(dve, T, 2, H, "o", done)
            dve.wait_ge(s["ro"], done)
            dve.wait_ge(s["gn"], done)
            for m in range(H):
                last = dve.scalar_tensor_tensor(out=o[0:T, m * P:(m + 1) * P], in0=pI[0:T, m * P:(m + 1) * P], scalar=rs[0:T, 2 + m:3 + m],
                                                in1=gs[0:T, m * P:(m + 1) * P], op0=ALU.mult, op1=ALU.mult)
            last.then_inc(s["o"], 1)
            dve.wait_ge(s["pool_mm"], done)
            for m in range(H):
                last = dve.tensor_scalar(mixT[:, n + m * T:n + (m + 1) * T], pV[:, m * T:(m + 1) * T], cols[:, 2 * H + m:2 * H + m + 1], None, ALU.mult)
            last.then_inc(s["pool_y"], 1)
            if sample:
                for j in range(NB):
                    dve.wait_ge(s["S_s_mm"], j + 1)
                    bank = (pG, pF)[j % 2]
                    for m in range(H):
                        c = m * NS + j * TS + TS - 1
                        dve.scalar_tensor_tensor(out=S0[:, j, m, :], in0=S0[:, j, m, :], scalar=eb[:, c:c + 1],
                                                 in1=bank[:, m * P:(m + 1) * P], op0=ALU.mult, op1=ALU.add).then_inc(s["S_s"], 1)
            for j, bank in enumerate((pW, pQ)):
                dve.wait_ge(s["out_mm"], 2 * t + j + 1)
                cut = slice(j * 512, (j + 1) * 512)
                dve.tensor_tensor(h[0:T, cut], bank[0:T, :], gate1[0:T, cut], ALU.mult).then_inc(s["gated"], 1)
                dve.wait_ge(s["gated"], 2 * t + j + 1)
                last = dve.tensor_tensor(x[0:T, cut], x[0:T, cut], h[0:T, cut], ALU.add)
            last.then_inc(s["x1"], 1)
            dve_norm(dve, T, 1, 1, "2", done)
            dve.wait_ge(s["r2"], done)
            for half in range(2):
                cut = slice(half * 512, (half + 1) * 512)
                dve.scalar_tensor_tensor(out=h[0:T, cut], in0=x[0:T, cut], scalar=rs[0:T, 1:2], in1=mul2[0:T, cut], op0=ALU.mult, op1=ALU.mult).then_inc(s["h20"], 1)
                dve.wait_ge(s["h20"], 2 * t + half + 1)
                dve.tensor_tensor(h[0:T, cut], h[0:T, cut], add2[0:T, cut], ALU.add).then_inc(s["h2"], 1)
            dve.wait_ge(s["h2T_ps"], 2 * t + 2)
            dve.tensor_copy(hT[:, 4 * T:8 * T], pB[:, 0:4 * T]).then_inc(s["h2T_hi"], 1)

        @block.vector
        def _(dve):
            dve.sem_inc(s["h2_out"], 16)
            dve.sem_inc(s["slotc_free"], 1)
            dve.wait_ge(s["cnt"], 1)
            dve.reciprocal(icnt[:, :, :], icnt[:, :, :]).then_inc(s["icnt_r"], 1)
            dve.memset(eps[:, :], EPS)
            dve.memset(A[:, :], 0.0)
            dve.memset(S[:, :], 0.0).then_inc(s["S"], 1)
            dve.wait_ge(s["cols_ps"], 1)
            dve.tensor_copy(cols[:, :], pA[:, 0:3 * H]).then_inc(s["cols"], 1)
            dve.wait_ge(s["cols"], 1)
            dve.tensor_tensor(lbd[:, :], cols[:, 0:H], cols[:, H:2 * H], ALU.subtract).then_inc(s["lbd"], 1)
            dve.wait_ge(s["lb"], 1)
            dve.tensor_scalar(oml[:, :], lb[:, :], -1.0, 1.0, ALU.mult, ALU.add)
            dve.wait_ge(s["rows_in"], 16 * 9)
            dve.scalar_tensor_tensor(out=mul1[:, :], in0=mul1[:, :], scalar=1.0, in1=x[:, :], op0=ALU.add, op1=ALU.mult)
            dve.scalar_tensor_tensor(out=mul2[:, :], in0=mul2[:, :], scalar=1.0, in1=h[:, :], op0=ALU.add, op1=ALU.mult).then_inc(s["x_free"], 1)
            dve.wait_ge(s["x_free"], 1)
            dve.wait_ge(s["consts"], 1)
            dve_tile(dve, 0, P, P, BLOCKS, False)
            with dve.Fori(1, TILES) as t:
                dve_tile(dve, t, P, P, BLOCKS, False)
            dve.wait_ge(s["rows_s"], 16 * (2 + 5 * NB))
            dve.scalar_tensor_tensor(out=mul1[0:NS, :], in0=mul1[0:NS, :], scalar=1.0, in1=x[0:NS, :], op0=ALU.add, op1=ALU.mult)
            dve.scalar_tensor_tensor(out=mul2[0:NS, :], in0=mul2[0:NS, :], scalar=1.0, in1=h[0:NS, :], op0=ALU.add, op1=ALU.mult).then_inc(s["rows_s_set"], 1)
            dve.wait_ge(s["rows_s_set"], 1)
            dve.memset(A[0:NS, 0:H * NS], 0.0)
            dve_tile(dve, TILES, NS, TS, BLOCKS_S, True)
            dve_route(dve, TILES, NS)

            M = ITEMS + 1
            dve.wait_ge(s["rank_used"], TILES + 1)
            cnt = pos
            dve.wait_ge(s["slotc"], TILES + 1)
            dve.tensor_tensor(cnt[:, :], slot0[:, :], region0[:, :], ALU.subtract).then_inc(s["im0"], 1)
            dve.wait_ge(s["im0"], 1)
            dve.tensor_scalar(im["m"][:, :], cnt[:, :], 0.0, None, ALU.is_gt).then_inc(s["im0"], 1)
            step = 2
            for c in range(1, REGION // ITEM):
                dve.tensor_scalar(im["t"][:, :], cnt[:, :], float(c * ITEM), None, ALU.is_gt).then_inc(s["im0"], 1)
                step += 1
                dve.wait_ge(s["im0"], step)
                dve.tensor_tensor(im["m"][:, :], im["m"][:, :], im["t"][:, :], ALU.add).then_inc(s["im0"], 1)
                step += 1
                dve.wait_ge(s["im0"], step)
            dve.tensor_tensor_scan(im["cum"][:, :], ones[:, 0:E], im["m"][:, :], 0.0, ALU.mult, ALU.add).then_inc(s["im1"], 1)
            dve.wait_ge(s["im1"], 1)
            dve.tensor_scalar(im["le"][0:M, :], im["cum"][0:M, :], iota_p[0:M, 0:1], None, ALU.is_le).then_inc(s["im1"], 1)
            dve.wait_ge(s["im1"], 2)
            dve.tensor_reduce(ic[0:M, 0:1], im["le"][0:M, :], AX, ALU.add)
            dve.tensor_tensor(im["lem"][0:M, :], im["le"][0:M, :], im["m"][0:M, :], ALU.mult).then_inc(s["im1"], 1)
            dve.wait_ge(s["im1"], 3)
            dve.tensor_reduce(ic[0:M, 1:2], im["lem"][0:M, :], AX, ALU.add)
            dve.tensor_scalar(im["hot"][0:M, :], iota_e[0:M, :], ic[0:M, 0:1], None, ALU.is_equal).then_inc(s["im1"], 1)
            dve.wait_ge(s["im1"], 4)
            dve.tensor_tensor(ic[0:M, 2:3], iota_p[0:M, 0:1], ic[0:M, 1:2], ALU.subtract)
            dve.tensor_tensor(im["hot"][0:M, :], im["hot"][0:M, :], cnt[0:M, :], ALU.mult).then_inc(s["im1"], 1)
            dve.wait_ge(s["im1"], 5)
            dve.tensor_reduce(ic[0:M, 3:4], im["hot"][0:M, :], AX, ALU.add)
            dve.tensor_scalar(ic[0:M, 4:5], ic[0:M, 2:3], float(ITEM), None, ALU.mult).then_inc(s["im1"], 1)
            dve.wait_ge(s["im1"], 6)
            dve.tensor_tensor(ic[0:M, 5:6], ic[0:M, 3:4], ic[0:M, 4:5], ALU.subtract).then_inc(s["im1"], 1)
            dve.wait_ge(s["im1"], 7)
            dve.scalar_tensor_tensor(out=ic[0:M, 6:7], in0=ic[0:M, 0:1], scalar=float(REGION), in1=ic[0:M, 4:5], op0=ALU.mult, op1=ALU.add)
            dve.tensor_scalar(ic[0:M, 7:8], ic[0:M, 0:1], float(E), float(IDLE), ALU.is_equal, ALU.mult)
            dve.tensor_scalar(ic[0:M, 8:9], ic[0:M, 5:6], float(SIZES[0]), None, ALU.is_gt).then_inc(s["im1"], 1)
            step = 8
            for size in SIZES[1:-1]:
                dve.wait_ge(s["im1"], step)
                dve.tensor_tensor(ic[0:M, 7:8], ic[0:M, 7:8], ic[0:M, 8:9], ALU.add).then_inc(s["im1"], 1)
                dve.wait_ge(s["im1"], step + 1)
                dve.tensor_scalar(ic[0:M, 8:9], ic[0:M, 5:6], float(size), None, ALU.is_gt).then_inc(s["im1"], 1)
                step += 2
            dve.wait_ge(s["im1"], step)
            dve.tensor_tensor(ic[0:M, 7:8], ic[0:M, 7:8], ic[0:M, 8:9], ALU.add).then_inc(s["im1"], 1)
            dve.wait_ge(s["im1"], step + 1)
            dve.tensor_copy(tab_f[:, 0:1], ic[0:M, 7:8])
            dve.tensor_scalar(tab_f[:, 1:2], ic[0:M, 0:1], float(E - 1), None, ALU.min)
            dve.tensor_scalar(tab_f[:, 2:3], ic[0:M, 6:7], float(SLOTS - ITEM), None, ALU.min).then_inc(s["items"], 1)

        def pool_route(pool, t, T):
            done = t + 1
            pool.wait_ge(s["slotc"], done)
            pool.sem_inc(s["met"], 1)
            for c in range(TOPK):
                pool.indirect_dma_start(scratch["slots"][:, :], bass.IndirectOffsetOnAxis(ap=slotc[0:T, c:c + 1], axis=0),
                                        entry[0:T, c, :], None).then_inc(s["listed"], 16)

        def pool_listed(pool, t):
            pool.wait_ge(s["listed"], 64 * t + 64)
            pool.sem_inc(s["slotc_free"], 1)

        def pool_tile(pool, t, T, G, blocks, sample):
            done = t + 1
            n = H * T
            if not first_tile(t):
                pool_route(pool, t - 1, P)
            pool.wait_ge(s["f"], done)
            pool.sem_inc(s["met"], 1)
            pool.tensor_scalar(k[:, 0:n], f[:, 0:n], -1.0, 1.0, ALU.mult, ALU.add).then_inc(s["k"], 1)
            pool.wait_ge(s["q"], done)
            pool.wait_ge(s["eb"], done)
            pool.tensor_tensor(qb[:, 0:n], q[:, 0:n], eb[:, 0:n], ALU.mult).then_inc(s["qb"], 1)
            pool.wait_ge(s["ek"], done)
            pool.wait_ge(s["k"], done)
            pool.tensor_tensor(kend[:, 0:n], k[:, 0:n], dk[:, 0:n], ALU.mult).then_inc(s["kend"], 1)
            level = t * (LV - 1)
            for i, B in enumerate(blocks):
                pool.wait_ge(s["elev"], level + i + 1)
                l, r, _ = halves(lev[i % 2][:, 0:n], B)
                kl, _, _ = halves(k[:, 0:n], B)
                _, qr, _ = halves(q[:, 0:n], B)
                pool.tensor_tensor(l, l, kl, ALU.mult)
                pool.tensor_tensor(r, r, qr, ALU.mult).then_inc(s["lev"], 1)
            pool.wait_ge(s["vx"], done)
            nb, tt = (NB, TS) if sample else (1, P)
            src = vxs if sample else vx[:, :, :].unsqueeze(2)
            bufs = (pw1, pw2)
            groups = []
            width = HIST + tt
            cur = src
            for g, w in enumerate(WINDOWS):
                sh = w // 2
                nw = width - sh
                dst = bufs[g % 2][:, 0:(H - g) * nb * nw].rearrange("p (h b t) -> p h b t", b=nb, t=nw)
                c = cur if g == 0 else cur[:, 1:]
                if g:
                    pool.wait_ge(s["win"], 4 * t + g)
                pool.tensor_tensor(dst, c[:, :, :, sh:width], c[:, :, :, 0:nw], ALU.add).then_inc(s["win"], 1)
                pool.wait_ge(s["win"], 4 * t + g + 1)
                d_out = wd[:, g * T:(g + 1) * T].rearrange("p (b t) -> p b t", b=nb)
                ic_v = icnt[:, g, 0:T].rearrange("p (b t) -> p b t", b=nb)
                pool.tensor_tensor(d_out, dst[:, 0, :, nw - tt:nw], ic_v, ALU.mult).then_inc(s["mean"], 1)
                cur, width = dst, nw
            pool.wait_ge(s["mean"], 4 * t + 4)
            pool.tensor_tensor(pw1[:, 0:n].rearrange("p (h b t) -> p h b t", h=H, b=nb), wd[:, 0:n].rearrange("p (h b t) -> p h b t", h=H, b=nb),
                               src[:, :, :, HIST:HIST + tt], ALU.subtract).then_inc(s["pool_d"], 1)
            if not sample:
                pool.wait_ge(s["pool_d"], done)
                pool.sem_inc(s["met"], 1)
                for g, w in enumerate(WINDOWS):
                    last = pool.memset(icnt[:, g, :], 1.0 / w)
                last.then_inc(s["icnt"], 1)
                pool.wait_ge(s["icnt"], done)
            pool.wait_ge(s["gs"], done)
            pool.tensor_tensor(gs[0:T, :], gs[0:T, :], hnorm[0:T, :], ALU.mult).then_inc(s["gn"], 1)
            if sample:
                pool.wait_ge(s["g_mm"], done)
                pool.memset(Qz, 0.0).then_inc(s["Qz0"], 1)
                pool.wait_ge(s["Qz0"], 1)
                pool.wait_ge(s["qb"], done)
                for j in range(NB):
                    last = pool.tensor_copy(Qz.rearrange("p (h b t) -> p h b t", h=H, b=NB)[:, :, j, j * TS:(j + 1) * TS],
                                            qb[:, 0:n].rearrange("p (h t) -> p h t", h=H)[:, :, j * TS:(j + 1) * TS])
                last.then_inc(s["Qz"], 1)
                pool.wait_ge(s["v"], done)
                for j in range(NB):
                    last = pool.tensor_scalar(Vz[:, j, :], v[0:NS, :], seqmask[:, j:j + 1], 0.0, ALU.mult, ALU.add)
                last.then_inc(s["Vz"], 1)
            if not first_tile(t):
                pool_listed(pool, t - 1)

        @block.gpsimd
        def _(pool):
            pool.memset(ident[:, :], 0.0)
            pool.memset(ones[:, :], 1.0)
            pool.memset(tri[:, :], 1.0)
            pool.memset(reset[:, :], 1.0)
            pool.memset(reset_s[:, :], 1.0)
            pool.memset(seqmask[:, :], 1.0)
            for m in masks:
                last = pool.memset(m[:, :], 0.0)
            last.then_inc(s["c0"], 1)
            pool.wait_ge(s["c0"], 1)
            pool.affine_select(out=ident[:, :], in_=ident[:, :], compare_op=ALU.not_equal, fill=1.0,
                               base=0, pattern=[[-1, P]], channel_multiplier=1)
            pool.affine_select(out=tri[:, :], in_=tri[:, :], compare_op=ALU.is_gt, fill=0.0,
                               base=0, pattern=[[1, P]], channel_multiplier=-1)
            pool.memset(reset[:, :].rearrange("p (h t) -> p h t", h=H)[:, :, 0:1], 0.0)
            pool.memset(reset_s[:, :].rearrange("p (g t) -> p g t", t=TS)[:, :, 0:1], 0.0)
            pool.affine_select(out=seqmask[:, :], in_=seqmask[:, :], compare_op=ALU.is_ge, fill=0.0,
                               base=0, pattern=[[-TS, NB]], channel_multiplier=1).then_inc(s["c0"], 1)
            pool.wait_ge(s["c0"], 2)
            pool.affine_select(out=seqmask[:, :], in_=seqmask[:, :], compare_op=ALU.is_ge, fill=0.0,
                               base=TS - 1, pattern=[[TS, NB]], channel_multiplier=-1)
            rights = [(B, m[:, :].rearrange("p (j two c) -> p j two c", two=2, c=B)[:, :, 1, :]) for B, m in zip(BLOCKS, masks)]
            for B, r in rights:
                last = pool.memset(r, 1.0)
            last.then_inc(s["c0"], 1)
            pool.wait_ge(s["c0"], 3)
            for B, r in rights:
                last = pool.affine_select(out=r, in_=r, compare_op=ALU.is_ge, fill=0.0, base=0,
                                          pattern=[[-2 * B, P // (2 * B)], [0, B]], channel_multiplier=1)
            last.then_inc(s["c0"], 1)
            pool.wait_ge(s["c0"], 4)
            for B, r in rights:
                last = pool.affine_select(out=r, in_=r, compare_op=ALU.is_ge, fill=0.0, base=B - 1,
                                          pattern=[[2 * B, P // (2 * B)], [0, B]], channel_multiplier=-1)
            pool.iota(iota_i[:, :], [[1, E]], base=0, channel_multiplier=0)
            pool.iota(entries[:, :, :, 0], [[P, TILES + 1], [0, TOPK]], base=0, channel_multiplier=1)
            pool.iota(entries[:, :, :, 1], [[P * TOPK, TILES + 1], [1, TOPK]], base=0, channel_multiplier=TOPK)
            pool.iota(iota_pi[:, :], [[0, 1]], base=0, channel_multiplier=1)
            pool.iota(ramp[:, :], [[1, P]], base=1, channel_multiplier=0).then_inc(s["c0"], 1)
            pool.memset(vx[:, :, :], 0.0).then_inc(s["c0"], 1)
            pool.wait_ge(s["c0"], 6)
            pool.tensor_copy(iota_e[:, :], iota_i[:, :])
            pool.tensor_copy(iota_p[:, :], iota_pi[:, :])
            pool.tensor_copy(wd[:, 0:P], ramp[:, :]).then_inc(s["c0"], 1)
            pool.wait_ge(s["c0"], 7)
            pool.tensor_scalar(slot0[:, :], iota_e[:, :], float(REGION), 0.0, ALU.mult, ALU.add)
            pool.tensor_scalar(region0[:, :], iota_e[:, :], float(REGION), 0.0, ALU.mult, ALU.add)
            for g, w in enumerate(WINDOWS):
                last = pool.tensor_scalar(icnt[:, g, :], wd[:, 0:P], float(w), 1.0, ALU.min, ALU.mult)
            last.then_inc(s["cnt"], 1)
            pool.wait_ge(s["icnt_r"], 1)
            pool.engine_nop().then_inc(s["consts"], 1)
            pool.sem_inc(s["carried"], 1)

            def prompt_tile(t):
                pool_tile(pool, t, P, P, BLOCKS, False)
                pool.tensor_copy(vx[:, :, 0:HIST], vx[:, :, P:P + HIST]).then_inc(s["carried"], 1)

            prompt_tile(0)
            with pool.Fori(1, TILES) as t:
                prompt_tile(t)
            pool_tile(pool, TILES, NS, TS, BLOCKS_S, True)
            pool_route(pool, TILES, NS)
            pool.wait_ge(s["listed"], 64 * (TILES + 1))
    s.clear()


def experts(nc, a, scratch):
    s = Signals(nc, "moe")
    UNITS, GU = FT + 4, FT
    PIECES, RAW = UNITS // 2, 3
    SPLIT, AHEAD, BANKS = 4, 3, 3
    with ExitStack() as ctx:
        def sb(name, shape, dt=F32):
            return ctx.enter_context(nc.sbuf_tensor(name, shape, dt))

        def ps(name):
            return ctx.enter_context(nc.psum_tensor(name, [P, 512], F32))

        raw = [sb(f"raw{j}", [P, 2, KT, 256]) for j in range(RAW)]
        hi = [sb(f"hi{j}", [P, 2, KT, P], F32R) for j in range(SPLIT)]
        lo = [sb(f"lo{j}", [P, 2, KT, P], F32R) for j in range(SPLIT)]
        table = sb("table", [1, (ITEMS + 1) * 3], I32)
        identm = sb("identm", [P, P])
        idx = sb("idx", [P, 2, 2], I32)
        dest = sb("dest", [P, 2], I32)
        xg = [sb(f"xg{m}", [P, D]) for m in range(2)]
        xs = sb("xs", [P, KT, 2, ITEM], F32R)
        brow = sb("brow", [2 * FT, P])
        bcol = sb("bcol", [P, 2 * FT])
        low = [[sb(f"low{j}{u}", [P, ITEM]) for u in range(2)] for j in range(2)]
        gate, sig, up, glu, act1 = ([sb(f"{n}{j}", [P, ITEM]) for j in range(2)] for n in ("gatem", "sigm", "upm", "glum", "actm"))
        acts = sb("acts", [P, FT, 2, ITEM], F32R)
        yT = sb("yT", [P, KT, ITEM])
        y = [sb(f"y{m}", [P, D]) for m in range(2)]
        pt = [ps("pt0"), ps("pt1")]
        pz = [[ps(f"pz{j}{u}").rearrange("p (h n) -> p h n", h=2) for u in range(2)] for j in range(BANKS)]
        block = ctx.enter_context(nc.Block())
        gu_view = a["w_gu"][0].rearrange("e (k p) (u n) -> e u p k n", p=P, u=2)
        dn_view = a["w_down"][0].rearrange("e (k p) (q n) -> e q p k n", p=P, n=256)
        bgu_view = a["b_gu"][0].rearrange("e (j p) -> e j p", p=P)

        def field(eng, i, c, top):
            return eng.value_load(table[0:1, bass.ds(i * 3 + c, 1)], min_val=0, max_val=top)

        def per_class(eng, body):
            with eng.Fori(0, ITEMS) as i:
                cls = field(eng, i, 0, IDLE)

                def choose(low, high):
                    if high - low == 1:
                        body(i, SIZES[low])
                        return
                    mid = (low + high) // 2
                    with eng.If(cls < mid):
                        choose(low, mid)
                    with eng.Else():
                        choose(mid, high)

                with eng.If(cls < IDLE):
                    choose(0, len(SIZES))

        def raw_unit(k):
            piece = raw[k // 2 % RAW]
            if k < GU:
                return piece[:, :, :, k % 2 * P:(k % 2 + 1) * P]
            return piece[:, k % 2, :, :].rearrange("p k (u n) -> p u k n", u=2)

        @block.sync
        def _(sp):
            sp.dma_start(table[:, :], scratch["table"].rearrange("i c -> (i c)").unsqueeze(0)).then_inc(s["table"], 16)
            sp.wait_ge(s["table"], 16)

            def load(e, q):
                for u in range(2):
                    src = (gu_view[bass.ds(e, 1), u, :, :, q * 256:(q + 1) * 256] if q < GU // 2
                           else dn_view[bass.ds(e, 1), 2 * q - GU + u])
                    sp.dma_start(raw[q % RAW][:, u, :, :], src.rearrange("o p k n -> (o p) k n")).then_inc(s[f"raw{q % RAW}"], 16)

            def load_bias(e):
                sp.dma_start(brow[:, :], bgu_view[bass.ds(e, 1)].rearrange("o j p -> (o j) p")).then_inc(s["brow"], 16)

            def load_slots(item):
                first = field(sp, item, 2, SLOTS - ITEM)
                for m in range(2):
                    sp.dma_start(idx[:, m, :], scratch["slots"][bass.ds(first + m * P, P), :]).then_inc(s["idx"], 16)

            load_slots(0)
            e0 = field(sp, 0, 1, E - 1)
            load_bias(e0)
            for q in range(RAW):
                if q == 1:
                    sp.wait_ge(s["xg"], 32)
                load(e0, q)
            with sp.Fori(0, ITEMS) as i:
                cls = field(sp, i, 0, IDLE)
                with sp.If(cls < IDLE):
                    e = field(sp, i, 1, E - 1)
                    e_next = field(sp, i + 1, 1, E - 1)
                    for q in range(RAW, PIECES + RAW):
                        sp.wait_ge(s["lo"], i * UNITS + 2 * (q - RAW) + 2)
                        load(e if q < PIECES else e_next, q % PIECES)
                        if q == RAW + 1:
                            sp.wait_ge(s["dest"], i + 1)
                            load_slots(i + 1)
                        if q == RAW:
                            sp.wait_ge(s["bcol_ps"], i + 1)
                            load_bias(e_next)
                    with sp.If(field(sp, i + 1, 0, IDLE) == IDLE):
                        for j in range(RAW):
                            sp.wait_ge(s[f"raw{j}"], i * 64 + 96)
                        sp.sem_inc(s["met"], 1)

        @block.gpsimd
        def _(pool):
            pool.memset(identm[:, :], 0.0).then_inc(s["ident0"], 1)
            pool.wait_ge(s["ident0"], 1)
            pool.affine_select(out=identm[:, :], in_=identm[:, :], compare_op=ALU.not_equal, fill=1.0,
                               base=0, pattern=[[-1, P]], channel_multiplier=1).then_inc(s["ident"], 1)

            def gather(item, m):
                pool.wait_ge(s["idx"], item * 32 + 32)
                pool.sem_inc(s["met"], 1)
                pool.indirect_dma_start(xg[m][:, :], None, scratch["h2"][:, :],
                                        bass.IndirectOffsetOnAxis(ap=idx[:, m, 0:1], axis=0)).then_inc(s["xg"], 16)

            def item(i, n):
                for j in range(GU + 1):
                    if j < GU:
                        c = j % 2
                        pool.wait_ge(s["read"], i * UNITS + j + 1 + BANKS)
                        pool.sem_inc(s["met"], 1)
                        pool.tensor_scalar(up[c][:, 0:n], up[c][:, 0:n], -LIMIT, LIMIT, ALU.max, ALU.min).then_inc(s["clip"], 1)
                        pool.wait_ge(s["sig"], i * GU + j + 1)
                        pool.tensor_tensor(glu[c][:, 0:n], gate[c][:, 0:n], sig[c][:, 0:n], ALU.mult).then_inc(s["glu"], 1)
                    if j:
                        c = j - 1
                        pool.wait_ge(s["ahi"], i * GU + c + 1)
                        pool.tensor_tensor(acts[:, c, 1, 0:n], act1[c % 2][:, 0:n], acts[:, c, 0, 0:n].bitcast(F32), ALU.subtract).then_inc(s["alo"], 1)
                    if j == 1:
                        pool.wait_ge(s["y_out"], i * 32 + 32)
                        pool.sem_inc(s["y_free"], 1)
                        pool.wait_ge(s["x_ps"], i * 4 + 4)
                        pool.sem_inc(s["met"], 1)
                        pool.tensor_copy(dest[:, :], idx[:, :, 1]).then_inc(s["dest"], 1)
                    if j in (3, 4):
                        gather(i + 1, j - 3)
                pool.wait_ge(s["dest"], i + 1)
                pool.wait_ge(s["y0"], 2 * i + 3)
                pool.wait_ge(s["y1"], 2 * i + 3)
                pool.sem_inc(s["met"], 1)
                for m, rows in enumerate((min(P, n), n - P)):
                    if rows > 0:
                        pool.indirect_dma_start(scratch["y"][:, :], bass.IndirectOffsetOnAxis(ap=dest[0:rows, m:m + 1], axis=0),
                                                y[m][0:rows, :], None, bounds_check=NT * TOPK - 1, oob_is_err=False)\
                            .then_inc(s["y_out"], 32 if n <= P else 16)
                with pool.If(field(pool, i + 1, 0, IDLE) == IDLE):
                    pool.wait_ge(s["y_out"], i * 32 + 64)
                    pool.sem_inc(s["met"], 1)

            pool.wait_ge(s["table"], 16)
            for m in range(2):
                gather(0, m)
            pool.dma_start(dest[:, :], scratch["slots"][0:P, :]).then_inc(s["y_out"], 32)
            pool.sem_inc(s["alo"], 2)
            per_class(pool, item)

        @block.tensor
        def _(pe):
            def transpose_rows(item, g):
                m, half = g // 2, g % 2
                if g == 0:
                    pe.wait_ge(s["xg"], item * 32 + 32)
                    if not first_tile(item):
                        pe.wait_ge(s["y0"], 2 * item - 1)
                        pe.wait_ge(s["y1"], 2 * item - 1)
                elif g > 1:
                    pe.wait_ge(s["xlo"], item * 4 + g - 1)
                for c in range(4):
                    last = pe.transpose(pt[half][:, c * P:(c + 1) * P], xg[m][:, (half * 4 + c) * P:(half * 4 + c + 1) * P], identm[:, :])
                last.then_inc(s["x_ps"], 1)

            def transpose_bias(item):
                pe.wait_ge(s["brow"], item * 16 + 16)
                pe.wait_ge(s["xlo"], item * 4 + 3)
                pe.sem_inc(s["met"], 1)
                pe.transpose(pt[0][:, 0:2 * FT], brow[:, :], identm[0:2 * FT, 0:2 * FT]).then_inc(s["bcol_ps"], 1)

            def product(k, u, kt, moving, n):
                bank, wh, wl = pz[k % BANKS][u], hi[k % SPLIT][:, u, kt, :], lo[k % SPLIT][:, u, kt, :]
                both = lambda: pe.matmul(bank[:, :, 0:n], wh, moving[:, kt, :, 0:n], start=(kt == 0), stop=(kt == KT - 1))
                if kt == 0:
                    both()
                last = pe.matmul(bank[:, 0, 0:n], wl, moving[:, kt, 0, 0:n], start=False, stop=False)
                return both() if kt else last

            def transpose_y(i, n, half):
                pe.wait_ge(s["read"], i * UNITS + GU + 2 * half + 2 + BANKS)
                pe.wait_ge(s["y0"], 2 * i + 2) if half else pe.wait_ge(s["bcol"], i + 2)
                pe.wait_ge(s["y1"], 2 * i + 2) if half else pe.wait_ge(s["xlo"], i * 4 + 8)
                for m, rows in enumerate((min(P, n), n - P)):
                    if rows > 0:
                        for c in range(4):
                            bank, at = (pt[m], c * P) if n > P else (pt[c // 2], c % 2 * P)
                            last = pe.transpose(bank[0:rows, at:at + P], yT[:, half * 4 + c, m * P:m * P + rows], identm[:, :])
                last.then_inc(s["y_ps"], 1)

            def item(i, n):
                for k in range(UNITS):
                    if k == 0:
                        pe.wait_ge(s["xlo"], i * 4 + 4)
                    if k == GU:
                        transpose_rows(i + 1, 0)
                        transpose_rows(i + 1, 1)
                        pe.wait_ge(s["alo"], i * GU + GU)
                    pe.wait_ge(s["lo"], i * UNITS + k + 1)
                    pe.wait_ge(s["read"], i * UNITS + k + 1)
                    moving = xs if k < GU else acts
                    if k == GU:
                        steps = [(u, kt) for u in range(2) for kt in range(KT - 2)] + [(u, kt) for kt in (KT - 2, KT - 1) for u in range(2)]
                    else:
                        steps = [(u, kt) for u in range(2) for kt in range(KT)]
                    for at, (u, kt) in enumerate(steps):
                        if k == GU and u == 0 and kt >= KT - 2:
                            pe.wait_ge(s["alo"], i * GU + kt + 3)
                        last = product(k, u, kt, moving, n)
                    last.then_inc(s["unit_mm"], 1)
                    if k == GU:
                        transpose_rows(i + 1, 2)
                        transpose_rows(i + 1, 3)
                    if k == GU + 1:
                        transpose_bias(i + 1)
                    if k == GU + 2:
                        transpose_y(i, n, 0)
                transpose_y(i, n, 1)

            pe.wait_ge(s["ident"], 1)
            pe.wait_ge(s["table"], 16)
            pe.sem_inc(s["unit_mm"], 1)
            for g in range(4):
                transpose_rows(0, g)
            transpose_bias(0)
            per_class(pe, item)

        @block.scalar
        def _(act):
            def split_hi(i, k):
                kk = k % UNITS
                q = kk // 2
                act.wait_ge(s[f"raw{q % RAW}"], (i + k // UNITS) * 64 + q // RAW * 32 + 32)
                if k >= AHEAD:
                    act.wait_ge(s["unit_mm"], i * UNITS + k - AHEAD + 1)
                act.activation(hi[kk % SPLIT][:, :, :, :], raw_unit(kk), ACT.Copy).then_inc(s["hi"], 1)

            def rows_hi(item, g):
                m, half = g // 2, g % 2
                act.wait_ge(s["x_ps"], item * 4 + g + 1)
                act.activation(xs[:, half * 4:half * 4 + 4, 0, m * P:(m + 1) * P], pt[half][:, :].rearrange("p (k t) -> p k t", k=4), ACT.Copy).then_inc(s["xhi"], 1)

            def act_hi(i, n, j):
                act.wait_ge(s["act"], i * GU + j + 1)
                act.activation(acts[:, j, 0, 0:n], act1[j % 2][:, 0:n], ACT.Copy).then_inc(s["ahi"], 1)

            def y_out(i, n, half):
                act.wait_ge(s["y_ps"], 2 * i + half + 1)
                if half == 0:
                    act.wait_ge(s["y_free"], i + 1)
                w = 512 if n > P else 256
                act.activation(y[0][0:min(P, n), half * 512:half * 512 + w], pt[0][0:min(P, n), 0:w], ACT.Copy).then_inc(s["y0"], 1)

            def item(i, n):
                for k in range(UNITS):
                    c = k % 2
                    if k == GU:
                        act_hi(i, n, GU - 1)
                        rows_hi(i + 1, 0)
                        rows_hi(i + 1, 1)
                    if k == GU + 1:
                        rows_hi(i + 1, 2)
                        rows_hi(i + 1, 3)
                    if k == UNITS - 1:
                        y_out(i, n, 0)
                    act.wait_ge(s["unit_mm"], i * UNITS + k + 2)
                    act.wait_ge(s["read"], i * UNITS + k - 1 + BANKS)
                    for u in range(2):
                        part, to = pz[k % BANKS][u][:, 1, 0:n], low[c][u][:, 0:n]
                        if k < GU:
                            act.activation(to, part, ACT.Identity, bias=bcol[:, u * FT + k:u * FT + k + 1]).then_inc(s[f"low{u}"], 1)
                        else:
                            act.activation(to, part, ACT.Copy).then_inc(s[f"low{u}"], 1)
                    if k != GU - 1:
                        split_hi(i, k + AHEAD)
                    if k < GU:
                        act.wait_ge(s["gate"], i * GU + k + 1)
                        act.activation(sig[c][:, 0:n], gate[c][:, 0:n], ACT.Sigmoid, scale=ALPHA).then_inc(s["sig"], 1)
                    if 1 <= k < GU:
                        act_hi(i, n, k - 1)
                    if k == GU - 1:
                        split_hi(i, k + AHEAD)
                y_out(i, n, 1)

            act.sem_inc(s["y0"], 1)
            act.wait_ge(s["table"], 16)
            for g in range(4):
                rows_hi(0, g)
            for k in range(AHEAD):
                split_hi(0, k)
            act.wait_ge(s["bcol"], 1)
            per_class(act, item)

        @block.vector
        def _(dve):
            def split_lo(i, k):
                kk = k % UNITS
                dve.wait_ge(s["hi"], i * UNITS + k + 1)
                dve.tensor_tensor(lo[kk % SPLIT][:, :, :, :], raw_unit(kk), hi[kk % SPLIT][:, :, :, :].bitcast(F32), ALU.subtract).then_inc(s["lo"], 1)

            def rows_lo(item, g):
                m, half = g // 2, g % 2
                dve.wait_ge(s["xhi"], item * 4 + g + 1)
                def part(h):
                    return xs[:, half * 4:half * 4 + 4, h, m * P:(m + 1) * P]

                dve.tensor_tensor(part(1), pt[half][:, :].rearrange("p (k t) -> p k t", k=4), part(0).bitcast(F32), ALU.subtract).then_inc(s["xlo"], 1)

            def bias_cols(item):
                dve.wait_ge(s["bcol_ps"], item + 1)
                dve.tensor_copy(bcol[:, :], pt[0][:, 0:2 * FT]).then_inc(s["bcol"], 1)
                dve.wait_ge(s["bcol"], item + 1)

            def finish(i, n, j):
                dve.wait_ge(s["clip"], i * GU + j + 1)
                dve.wait_ge(s["glu"], i * GU + j + 1)
                dve.wait_ge(s["alo"], i * GU + j + 1)
                dve.scalar_tensor_tensor(out=act1[j % 2][:, 0:n], in0=up[j % 2][:, 0:n], scalar=1.0, in1=glu[j % 2][:, 0:n],
                                         op0=ALU.add, op1=ALU.mult).then_inc(s["act"], 1)

            def y_out(i, n, half):
                dve.wait_ge(s["y_ps"], 2 * i + half + 1)
                if half == 0:
                    dve.wait_ge(s["y_free"], i + 1)
                if n > P:
                    dve.tensor_copy(y[1][0:n - P, half * 512:(half + 1) * 512], pt[1][0:n - P, :]).then_inc(s["y1"], 1)
                else:
                    dve.tensor_copy(y[0][0:n, half * 512 + 256:(half + 1) * 512], pt[1][0:n, 0:256]).then_inc(s["y1"], 1)

            def item(i, n):
                for k in range(UNITS):
                    if k == GU:
                        finish(i, n, GU - 1)
                        rows_lo(i + 1, 0)
                        rows_lo(i + 1, 1)
                    if k == GU + 1:
                        rows_lo(i + 1, 2)
                        rows_lo(i + 1, 3)
                    if k == GU + 2:
                        bias_cols(i + 1)
                    if k == UNITS - 1:
                        y_out(i, n, 0)
                    c, gu = k % 2, k < GU
                    bank0, bank1 = pz[k % BANKS]
                    to0, to1 = (gate[c], up[c]) if gu else (yT[:, 2 * (k - GU), :], yT[:, 2 * (k - GU) + 1, :])
                    dve.wait_ge(s["low0"], i * UNITS + k + 1)
                    dve.tensor_tensor(to0[:, 0:n], bank0[:, 0, 0:n], low[c][0][:, 0:n], ALU.add).then_inc(s["add0"], 1)
                    dve.wait_ge(s["low1"], i * UNITS + k + 1)
                    dve.tensor_tensor(to1[:, 0:n], bank1[:, 0, 0:n], low[c][1][:, 0:n], ALU.add).then_inc(s["read"], 1)
                    if gu:
                        dve.wait_ge(s["add0"], i * UNITS + k + 1)
                        dve.tensor_scalar(gate[c][:, 0:n], gate[c][:, 0:n], LIMIT, None, ALU.min).then_inc(s["gate"], 1)
                    if 1 <= k < GU:
                        finish(i, n, k - 1)
                    split_lo(i, k + AHEAD - 1)
                y_out(i, n, 1)

            dve.sem_inc(s["read"], BANKS)
            dve.sem_inc(s["y1"], 1)
            dve.wait_ge(s["table"], 16)
            for g in range(4):
                rows_lo(0, g)
            for k in range(AHEAD - 1):
                split_lo(0, k)
            bias_cols(0)
            per_class(dve, item)

    s.clear()


def combination(nc, a, scratch, out, keep):
    with ExitStack() as ctx:
        def sb(name, shape, dt=F32):
            return ctx.enter_context(nc.sbuf_tensor(name, shape, dt))

        def two(name, shape, dt=F32):
            return [sb(f"{name}{j}", shape, dt) for j in range(2)]

        s = Signals(nc, "cmb")
        probs, pdense, ident = keep["probs"], keep["pdense"], keep["ident"]
        gate2, gate2_s, fnorm = sb("gate2", [P, D]), sb("gate2_s", [NS, D]), sb("fnorm", [P, D])
        bdown = sb("bdown", [E, D])
        eps = sb("epsc", [P, 1])
        pr, pd, pT = two("pr", [P, TOPK]), two("pd", [P, E]), two("pT", [E, P])
        yk = two("yk", [P, TOPK, D])
        x1, acc, res, sq = two("x1c", [P, D]), two("acc", [P, D]), two("res", [P, D]), sb("sq", [P, D])
        ss, r = two("ssc", [P, 1]), two("rc", [P, 1])
        ppT = [ctx.enter_context(nc.psum_tensor(f"ppT{j}", [P, 512], F32)) for j in range(2)]
        pb = [[ctx.enter_context(nc.psum_tensor(f"pb{j}{c}", [P, 512], F32)) for c in range(2)] for j in range(2)]
        block = ctx.enter_context(nc.Block())

        PAIRS = TILES // 2

        def all_tiles(eng, body, T_last=NS):
            with eng.Fori(0, PAIRS) as i:
                for u in range(2):
                    body(i, u, P, i * 2 + u, False)
            body(PAIRS, 0, T_last, TILES, True)

        def all_tiles_lagged(eng, first, second):
            def each(part, i, u, sample=False):
                part(i, u, NS if sample else P, TILES if sample else i * 2 + u, sample)

            each(first, 0, 0)
            with eng.Fori(0, PAIRS - 1) as i:
                each(first, i, 1)
                each(second, i, 0)
                each(first, i + 1, 0)
                each(second, i, 1)
            each(first, PAIRS - 1, 1)
            each(second, PAIRS - 1, 0)
            each(first, PAIRS, 0, True)
            each(second, PAIRS - 1, 1)
            each(second, PAIRS, 0, True)

        def pick(ap, t, T):
            return ap[0:T, t:t + 1, :] if isinstance(t, int) else ap[0:T, bass.ds(t, 1), :]

        @block.sync
        def _(sp):
            sp.dma_start(gate2[:, :], scratch["mod"][0:1, G2 * D:].broadcast_to([P, D])).then_inc(s["rows"], 16)
            for j in range(NB):
                sp.dma_start(gate2_s[j * TS:(j + 1) * TS, :], scratch["mod"][1 + j:2 + j, G2 * D:].broadcast_to([TS, D])).then_inc(s["rows"], 16)
            sp.dma_start(fnorm[:, :], a["final_norm"].unsqueeze(0).broadcast_to([P, D])).then_inc(s["rows"], 16)
            sp.dma_start(bdown[:, :], a["b_down"][0]).then_inc(s["rows"], 16)

            def tile(i, u, T, t, sample):
                sp.wait_ge(s[f"sum{u}"], i + 1)
                rows = scratch["y"].rearrange("(t c) d -> t (c d)", c=TOPK)
                sp.dma_start(yk[u][0:T, :, :].rearrange("p c d -> p (c d)"), rows[NTOK:NT, :] if sample else rows[bass.ds(t * P, P), :]).then_inc(s[f"yk{u}"], 16)
                src = scratch["x1"][NTOK:NT, :] if sample else scratch["x1"][bass.ds(t * P, P), :]
                sp.dma_start(x1[u][0:T, :], src).then_inc(s[f"x1{u}"], 16)

            all_tiles(sp, tile)

        @block.gpsimd
        def _(pool):
            for u in range(2):
                pool.sem_inc(s[f"sum{u}"], 1)

            def tile(i, u, T, t, sample):
                g = gate2_s if sample else gate2
                pool.wait_ge(s["rows"], 16 * (NB + 3))
                pool.wait_ge(s[f"weighed{u}"], i + 1)
                pool.tensor_tensor(acc[u][0:T, :], acc[u][0:T, :], g[0:T, :], ALU.mult).then_inc(s[f"gated{u}"], 1)
                pool.wait_ge(s[f"gated{u}"], i + 1)
                pool.wait_ge(s[f"x1{u}"], i * 16 + 16)
                pool.tensor_tensor(acc[u][0:T, :], acc[u][0:T, :], x1[u][0:T, :], ALU.add).then_inc(s[f"sum{u}"], 1)

            all_tiles(pool, tile)

        @block.tensor
        def _(pe):
            pe.wait_ge(s["rows"], 16 * (NB + 3))

            def tile(i, u, T, t, sample):
                pe.wait_ge(s[f"picked{u}"], i + 1)
                pe.transpose(ppT[u][0:E, 0:T], pd[u][0:T, :], ident[0:T, 0:T]).then_inc(s[f"pT_ps{u}"], 1)
                pe.wait_ge(s[f"pT{u}"], i + 1)
                for c in range(2):
                    last = pe.matmul(pb[u][c][0:T, :], pT[u][:, 0:T], bdown[:, c * 512:(c + 1) * 512], start=True, stop=True)
                last.then_inc(s[f"bias{u}"], 1)

            all_tiles(pe, tile)

        @block.scalar
        def _(act):
            for u in range(2):
                act.sem_inc(s[f"out{u}"], 16)

            def tile(i, u, T, t, sample):
                act.wait_ge(s[f"pT_ps{u}"], i + 1)
                act.activation(pT[u][:, 0:T], ppT[u][0:E, 0:T], ACT.Copy).then_inc(s[f"pT{u}"], 1)

            def norm(i, u, T, t, sample):
                act.wait_ge(s["epsc"], 1)
                act.wait_ge(s[f"sum{u}"], i + 2)
                act.activation(sq[0:T, :], acc[u][0:T, :], ACT.Square, accum_out=ss[u][0:T, :]).then_inc(s[f"ss{u}"], 1)
                act.wait_ge(s[f"ss{u}"], i + 1)
                act.activation(r[u][0:T, :], ss[u][0:T, :], ACT.Sqrt, scale=1.0 / D, bias=eps[0:T, :]).then_inc(s[f"root{u}"], 1)
                act.wait_ge(s[f"res{u}"], i + 1)
                dst = out["y_s"].rearrange("b t d -> (b t) d") if sample else out["y_p"][0, bass.ds(t * P, P), :]
                act.dma_start(dst, res[u][0:T, :]).then_inc(s[f"out{u}"], 16)

            all_tiles_lagged(act, tile, norm)
            act.wait_ge(s["out0"], 16 * (PAIRS + 2))
            act.wait_ge(s["out1"], 16 * (PAIRS + 1))

        @block.vector
        def _(dve):
            dve.memset(eps[:, :], EPS).then_inc(s["epsc"], 1)
            dve.wait_ge(s["rows"], 16 * (NB + 3))

            def tile(i, u, T, t, sample):
                dve.tensor_copy(pr[u][0:T, :].unsqueeze(1), pick(probs, t, T))
                dve.tensor_copy(pd[u][0:T, :].unsqueeze(1), pick(pdense, t, T)).then_inc(s[f"picked{u}"], 1)
                dve.wait_ge(s[f"picked{u}"], i + 1)
                dve.wait_ge(s[f"bias{u}"], i + 1)
                dve.wait_ge(s[f"yk{u}"], i * 16 + 16)
                for c in range(2):
                    last = dve.scalar_tensor_tensor(out=acc[u][0:T, c * 512:(c + 1) * 512], in0=yk[u][0:T, 0, c * 512:(c + 1) * 512], scalar=pr[u][0:T, 0:1],
                                                    in1=pb[u][c][0:T, :], op0=ALU.mult, op1=ALU.add)
                last.then_inc(s[f"part{u}"], 1)
                for c in range(1, TOPK):
                    dve.wait_ge(s[f"part{u}"], i * (TOPK - 1) + c)
                    last = dve.scalar_tensor_tensor(out=acc[u][0:T, :], in0=yk[u][0:T, c, :], scalar=pr[u][0:T, c:c + 1],
                                                    in1=acc[u][0:T, :], op0=ALU.mult, op1=ALU.add)
                    last.then_inc(s[f"part{u}" if c < TOPK - 1 else f"weighed{u}"], 1)

            def norm(i, u, T, t, sample):
                dve.wait_ge(s[f"root{u}"], i + 1)
                dve.reciprocal(r[u][0:T, :], r[u][0:T, :]).then_inc(s[f"r{u}"], 1)
                dve.wait_ge(s[f"r{u}"], i + 1)
                dve.wait_ge(s[f"out{u}"], i * 16 + 16)
                dve.scalar_tensor_tensor(out=res[u][0:T, :], in0=acc[u][0:T, :], scalar=r[u][0:T, 0:1], in1=fnorm[0:T, :],
                                         op0=ALU.mult, op1=ALU.mult).then_inc(s[f"res{u}"], 1)

            all_tiles_lagged(dve, tile, norm)


def build(nc, a, out):
    def dram(name, shape, dt=F32):
        return nc.dram_tensor(name, shape, dt, kind="Internal").ap()

    scratch = {
        "mod": dram("mod", (NC, MODS * D)),
        "x1": dram("x1_rows", (NT, D)),
        "h2": dram("h2_rows", (NT, D)),
        "slots": dram("slots", (SLOTS, 2), I32),
        "table": dram("item_table", (ITEMS + 1, 3), I32),
        "y": dram("expert_rows", (NT * TOPK, D)),
    }
    with ExitStack() as ctx:
        keep = {
            "probs": ctx.enter_context(nc.sbuf_tensor("probs", [P, TILES + 1, TOPK], F32)),
            "pdense": ctx.enter_context(nc.sbuf_tensor("pdense", [P, TILES + 1, E], F32)),
            "ident": ctx.enter_context(nc.sbuf_tensor("ident", [P, P], F32)),
        }
        modulation(nc, a, scratch)
        mixing(nc, a, scratch, out, keep)
        experts(nc, a, scratch)
        combination(nc, a, scratch, out, keep)


OUTPUTS = {
    "y_p": (1, NTOK, D), "y_s": (NB, TS, D), "S_p": (1, 1, H, P, P), "H_p": (1, 1, HIST, HW),
    "S_s": (1, NB, H, P, P), "H_s": (1, NB, HIST, HW),
}


def kernel(**inputs):
    import numpy as np
    import concourse.bacc as bacc
    from concourse.bass_utils import run_bass_kernel_spmd

    nc = bacc.Bacc("TRN2", target_bir_lowering=False, num_devices=1)
    arrays, a = {}, {}
    for name, value in inputs.items():
        arrays["in_" + name] = np.ascontiguousarray(value)
        a[name] = nc.dram_tensor("in_" + name, arrays["in_" + name].shape, F32, kind="ExternalInput").ap()
    out = {name: nc.dram_tensor("out_" + name, shape, F32, kind="ExternalOutput").ap() for name, shape in OUTPUTS.items()}
    build(nc, a, out)
    r = run_bass_kernel_spmd(nc, [arrays], core_ids=[0]).results[0]
    return tuple(r["out_" + name] for name in OUTPUTS)
```
